# Optimizing a Trainium2 kernel written in Bass

```python
import math
import jax, jax.numpy as jnp
from jax import lax
import numpy as np

D_MODEL = 1024
BATCH = 1
SEQ = 512
DEPTH = 1

CHUNK = 64
Q_BLOCK = 128

FOX_HEADS = 8
FOX_HEAD_DIM = 64
FOX_WIDTH = FOX_HEADS * FOX_HEAD_DIM

DIFF_HEADS = 4
DIFF_HALF_DIM = 64
DIFF_HEAD_DIM = 2 * DIFF_HALF_DIM
DIFF_WIDTH = DIFF_HEADS * DIFF_HEAD_DIM

MIX_WIDTH = FOX_WIDTH + DIFF_WIDTH
IN_COLS = 3 * FOX_WIDTH + FOX_HEADS + 3 * DIFF_WIDTH

PEER_HEADS = 8
PEER_N_KEYS = 128
PEER_N_EXPERTS = PEER_N_KEYS * PEER_N_KEYS
PEER_HALF_DIM = 128
PEER_QUERY_DIM = 2 * PEER_HALF_DIM
PEER_TOPK = 16
PEER_TOKEN_BLOCK = 128

RMS_EPS = 1e-6

kernel_name = "hybrid_fox_diffattn_peer_block"

def _rmsnorm(x, g):
    xf = x.astype(jnp.float32)
    y = xf * lax.rsqrt(jnp.mean(xf * xf, axis=-1, keepdims=True) + RMS_EPS)
    return (y * g.astype(jnp.float32)).astype(x.dtype)

def _alibi_slopes(n):
    return jnp.asarray([2.0 ** (-8.0 * (i + 1) / n) for i in range(n)], dtype=jnp.float32)

def _sweep(body, n_blocks):
    out = lax.map(body, jnp.arange(n_blocks))
    nb, b, h, qb, dv = out.shape
    return out.transpose(1, 0, 3, 2, 4).reshape(b, nb * qb, h * dv)

def _forgetting_attention(q, k, v, log_f):
    seq = q.shape[2]
    scale = FOX_HEAD_DIM ** -0.5
    c = jnp.cumsum(log_f, axis=-1)
    key_pos = jnp.arange(seq)

    def body(i):
        start = i * Q_BLOCK
        qb = lax.dynamic_slice_in_dim(q, start, Q_BLOCK, axis=2)
        cq = lax.dynamic_slice_in_dim(c, start, Q_BLOCK, axis=2)
        t = start + jnp.arange(Q_BLOCK)
        logits = (jnp.einsum('bhqd,bhkd->bhqk', qb, k).astype(jnp.float32) * scale
                  + (cq[..., :, None] - c[..., None, :]))
        mask = key_pos[None, :] <= t[:, None]
        p = jax.nn.softmax(jnp.where(mask, logits, -jnp.inf), axis=-1)
        return jnp.einsum('bhqk,bhkd->bhqd', p.astype(v.dtype), v)

    return _sweep(body, seq // Q_BLOCK)

def _differential_attention(q1, k1, q2, k2, v, lam, lambda_init, subln_g):
    seq = q1.shape[2]
    scale = DIFF_HALF_DIM ** -0.5
    slopes = _alibi_slopes(DIFF_HEADS)
    key_pos = jnp.arange(seq)

    def body(i):
        start = i * Q_BLOCK
        q1b = lax.dynamic_slice_in_dim(q1, start, Q_BLOCK, axis=2)
        q2b = lax.dynamic_slice_in_dim(q2, start, Q_BLOCK, axis=2)
        t = start + jnp.arange(Q_BLOCK)
        dist = jnp.abs(t[:, None] - key_pos[None, :]).astype(jnp.float32)
        alibi = -slopes[:, None, None] * dist[None]
        mask = (key_pos[None, :] // CHUNK) <= (t[:, None] // CHUNK)
        l1 = jnp.einsum('bhqd,bhkd->bhqk', q1b, k1).astype(jnp.float32) * scale + alibi
        l2 = jnp.einsum('bhqd,bhkd->bhqk', q2b, k2).astype(jnp.float32) * scale + alibi
        a1 = jax.nn.softmax(jnp.where(mask, l1, -jnp.inf), axis=-1)
        a2 = jax.nn.softmax(jnp.where(mask, l2, -jnp.inf), axis=-1)
        attn = a1 - lam * a2
        o = jnp.einsum('bhqk,bhkd->bhqd', attn.astype(v.dtype), v)
        return _rmsnorm(o, subln_g) * (1.0 - lambda_init)

    return _sweep(body, seq // Q_BLOCK)

def _peer(xn, w_q, sub_keys, u_tab, v_tab):
    b, s, d = xn.shape
    blocks = xn.reshape(-1, PEER_TOKEN_BLOCK, d)

    def body(xb):
        q = (xb @ w_q).reshape(PEER_TOKEN_BLOCK, PEER_HEADS, 2, PEER_HALF_DIM)
        sc = jnp.einsum('thpd,hpkd->thpk', q, sub_keys).astype(jnp.float32)
        s1, i1 = lax.top_k(sc[:, :, 0], PEER_TOPK)
        s2, i2 = lax.top_k(sc[:, :, 1], PEER_TOPK)
        cand = (s1[..., :, None] + s2[..., None, :]).reshape(PEER_TOKEN_BLOCK, PEER_HEADS, -1)
        cidx = (i1[..., :, None] * PEER_N_KEYS + i2[..., None, :]).reshape(PEER_TOKEN_BLOCK, PEER_HEADS, -1)
        top_s, pos = lax.top_k(cand, PEER_TOPK)
        eidx = jnp.take_along_axis(cidx, pos, axis=-1)
        g = jax.nn.softmax(top_s, axis=-1).astype(xb.dtype)
        u_sel = jnp.take(u_tab, eidx, axis=0)
        hid = jax.nn.gelu(jnp.einsum('thkd,td->thk', u_sel, xb), approximate=False) * g
        v_sel = jnp.take(v_tab, eidx, axis=0)
        return jnp.einsum('thk,thkd->td', hid, v_sel)

    return lax.map(body, blocks).reshape(b, s, d)

def setup_inputs(seed: int = 0) -> dict:
    key = jax.random.key(seed)
    ks = jax.random.split(key, 17)
    f32 = jnp.float32
    n = lambda k, shape, sc: jax.random.normal(k, shape, f32) * sc
    return {
        "x": n(ks[0], (BATCH, SEQ, D_MODEL), 1.0),
        "norm1_g": 1.0 + n(ks[1], (DEPTH, D_MODEL), 0.02),
        "w_in": n(ks[2], (DEPTH, D_MODEL, IN_COLS), D_MODEL ** -0.5),
        "b_f": 2.5 + n(ks[3], (DEPTH, FOX_HEADS), 0.5),
        "lambda_q1": n(ks[4], (DEPTH, DIFF_HALF_DIM), 0.1),
        "lambda_k1": n(ks[5], (DEPTH, DIFF_HALF_DIM), 0.1),
        "lambda_q2": n(ks[6], (DEPTH, DIFF_HALF_DIM), 0.1),
        "lambda_k2": n(ks[7], (DEPTH, DIFF_HALF_DIM), 0.1),
        "subln_g": 1.0 + n(ks[8], (DEPTH, DIFF_HEAD_DIM), 0.02),
        "w_out": n(ks[9], (DEPTH, MIX_WIDTH, D_MODEL), MIX_WIDTH ** -0.5),
        "norm2_g": 1.0 + n(ks[10], (DEPTH, D_MODEL), 0.02),
        "peer_w_q": n(ks[11], (DEPTH, D_MODEL, PEER_HEADS * PEER_QUERY_DIM), D_MODEL ** -0.5),
        "peer_sub_keys": n(ks[12], (DEPTH, PEER_HEADS, 2, PEER_N_KEYS, PEER_HALF_DIM), PEER_HALF_DIM ** -0.5),
        "peer_u": n(ks[13], (DEPTH, PEER_N_EXPERTS, D_MODEL), D_MODEL ** -0.5),
        "peer_v": n(ks[14], (DEPTH, PEER_N_EXPERTS, D_MODEL), 0.5),
        "final_g": 1.0 + n(ks[15], (D_MODEL,), 0.02),
    }

def reference(x, norm1_g, w_in, b_f, lambda_q1, lambda_k1, lambda_q2, lambda_k2,
              subln_g, w_out, norm2_g, peer_w_q, peer_sub_keys, peer_u, peer_v, final_g):
    b, s, _ = x.shape
    split_pts = np.cumsum([FOX_WIDTH, FOX_WIDTH, FOX_WIDTH, FOX_HEADS, DIFF_WIDTH, DIFF_WIDTH])
    h = x
    for layer in range(DEPTH):
        xn = _rmsnorm(h, norm1_g[layer])
        proj = xn @ w_in[layer]
        qa, ka, va, fa, qb, kb, vb = jnp.split(proj, split_pts, axis=-1)

        heads_a = lambda t: t.reshape(b, s, FOX_HEADS, FOX_HEAD_DIM).transpose(0, 2, 1, 3)
        log_f = jax.nn.log_sigmoid((fa + b_f[layer]).astype(jnp.float32)).transpose(0, 2, 1)
        out_a = _forgetting_attention(heads_a(qa), heads_a(ka), heads_a(va), log_f)

        heads_b = lambda t: t.reshape(b, s, DIFF_HEADS, DIFF_HEAD_DIM).transpose(0, 2, 1, 3)
        qb_h, kb_h, vb_h = heads_b(qb), heads_b(kb), heads_b(vb)
        lambda_init = 0.8 - 0.6 * math.exp(-0.3 * layer)
        lam = (jnp.exp(jnp.sum(lambda_q1[layer].astype(jnp.float32) * lambda_k1[layer].astype(jnp.float32)))
               - jnp.exp(jnp.sum(lambda_q2[layer].astype(jnp.float32) * lambda_k2[layer].astype(jnp.float32)))
               + lambda_init)
        out_b = _differential_attention(
            qb_h[..., :DIFF_HALF_DIM], kb_h[..., :DIFF_HALF_DIM],
            qb_h[..., DIFF_HALF_DIM:], kb_h[..., DIFF_HALF_DIM:],
            vb_h, lam, lambda_init, subln_g[layer])

        mixed = jnp.concatenate([out_a, out_b], axis=-1)
        h = h + mixed @ w_out[layer]

        hn = _rmsnorm(h, norm2_g[layer])
        h = h + _peer(hn, peer_w_q[layer], peer_sub_keys[layer], peer_u[layer], peer_v[layer])
    return _rmsnorm(h, final_g)


_drawn_inputs = setup_inputs


def setup_inputs(seed=0):
    import zlib

    import numpy as np

    out = dict(_drawn_inputs(seed))
    spreads = {}
    factors = {}
    for name, (base, spread) in spreads.items():
        noise = np.random.default_rng([zlib.crc32(name.encode()), seed]).standard_normal(out[name].shape)
        drawn = base * np.exp(spread * noise) if base else spread * noise
        out[name] = __import__('jax').numpy.asarray(drawn.astype(out[name].dtype))
    for name, factor in factors.items():
        out[name] = (out[name] * factor).astype(out[name].dtype)
    return out
```

```python
import math
from contextlib import ExitStack

import concourse.bass as bass
from concourse import mybir

F32 = mybir.dt.float32
I32 = mybir.dt.int32
U32 = mybir.dt.uint32
ALU = mybir.AluOpType
ACT = mybir.ActivationFunctionType
AX = mybir.AxisListType.X

P = 128
HALF_BANK = 256
BANK = 512
EPS = 1e-6
BIG = 1e30
HUGE = 3e38
LAMBDA_INIT = 0.8 - 0.6 * math.exp(-0.3 * 0)

GROUPS = [[0], [1], [2, 3]]
HOST_TILES = {1: 0, 2: 1}
COLS = 4
U_RING = 4
V_RING = 4
V_ON_VECTOR = [1, 2, 0, 0]
W_RING = 2
S_RING = 6


def build(nc, x, norm1_g, w_in, b_f, lambda_q1, lambda_k1, lambda_q2, lambda_k2, subln_g, w_out,
          norm2_g, peer_w_q, peer_sub_keys, peer_u, peer_v, final_g, out):
    _, SEQ, D = x.shape
    KC = D // P
    FH = b_f.shape[1]
    HD = lambda_q1.shape[1]
    DH = subln_g.shape[1]
    NDH = D // 2 // DH
    FW = FH * HD
    TILES = SEQ // P
    PH, K1 = peer_sub_keys.shape[1], peer_sub_keys.shape[3]
    TOPK = 16
    SLAB = HALF_BANK
    CHUNK = 64
    slopes = [2.0 ** (-8.0 * (i + 1) / NDH) for i in range(NDH)]
    HEADS = TILES * PH
    SC_TILES = 3
    max_n = P * max(len(g) for g in GROUPS)

    in_kinds = []
    for kind, base in (("qa", 0), ("ka", FW), ("va", 2 * FW),
                       ("qb", 3 * FW + FH), ("kb", 4 * FW + FH), ("vb", 5 * FW + FH)):
        for c in range(0, FW, SLAB):
            in_kinds.append((kind, base + c, c))
    slab_src = ([w_in[0][:, c:c + SLAB] for _, c, _ in in_kinds]
                + [w_out[0][:, c:c + SLAB] for c in range(0, D, SLAB)]
                + [peer_w_q[0][:, c:c + SLAB] for c in range(0, PH * 2 * P, SLAB)])
    N_IN, N_OUT = len(in_kinds), D // SLAB
    SLABS = len(slab_src)

    ITEMS = FH + NDH
    MAPS = FH + 2 * NDH

    def maps_of(item):
        return [item] if item < FH else [FH + 2 * (item - FH), FH + 2 * (item - FH) + 1]

    def item_of(m):
        return m if m < FH else FH + (m - FH) // 2

    STEPS = ITEMS + 3

    def pieces_of(g):
        ps = [("norm1", g, t) for t in GROUPS[g]]
        ps += [("project", g, s) for s in range(4)] + [("forget", g, 0)]
        if g == 0:
            ps += [("lambda", 0, 0)]
        ps += [("project", g, s) for s in range(4, N_IN)]
        for t in GROUPS[g]:
            ps += [("attend", t, s) for s in range(STEPS)] + [("mix", g, t)]
        ps += [("outproj", g, s) for s in range(N_OUT)]
        ps += [("norm2", g, t) for t in GROUPS[g]]
        if g == 0:
            ps += [("subkeys", 0, 0)]
        ps += [("query", g, s) for s in range(PH + 1)]
        return ps

    PIECES = [pieces_of(g) for g in range(len(GROUPS))]

    MM = [("gain1",)]
    slab_last_use = []
    for g, ps in enumerate(PIECES):
        for kind, a, b in ps:
            if kind == "norm1":
                MM += [("xT", b, h) for h in range(2)]
            elif kind == "forget":
                MM.append(("forget", g))
            elif kind == "lambda":
                MM.append(("lambda",))
            elif kind == "subkeys":
                MM += [("subkeys", i) for i in range(2 * PH // 4)]
            elif kind == "project":
                if in_kinds[b][0] in ("va", "vb"):
                    MM += [("v", b, t) for t in GROUPS[g]]
                else:
                    MM += [("qk", g, b, c) for c in range(2)]
                slab_last_use.append(len(MM) - 1)
            elif kind == "mix":
                MM += [("mixT", b, h) for h in range(2)]
            elif kind == "outproj":
                MM += [("out", b, t) for t in GROUPS[g]]
                slab_last_use.append(len(MM) - 1)
            elif kind == "norm2":
                MM += [("hT", b, h) for h in range(2)]
            elif kind == "query":
                if b < PH:
                    MM.append(("query", g, 2 * b))
                if b > 0:
                    MM += [("keys", b - 1, t) for t in GROUPS[g]]
                if b < PH:
                    MM.append(("query", g, 2 * b + 1))
                    slab_last_use.append(len(MM) - 1)
    mm_no = {name: i for i, name in enumerate(MM)}

    xs_no, xs_prev, reader = {}, {}, None
    for ps in PIECES:
        for kind, _, t in ps:
            if kind in ("norm1", "mix", "norm2"):
                xs_no[(kind, t)] = len(xs_no) + 1
                xs_prev[(kind, t)] = reader
                if kind != "mix":
                    reader = ("xT" if kind == "norm1" else "hT", t, 1)

    def mm_done(name):
        return mm_no[name] + 1

    with ExitStack() as ctx:
        def sb(name, shape, dt=F32):
            return ctx.enter_context(nc.sbuf_tensor(name, shape, dt))

        def sem(name):
            return ctx.enter_context(nc.semaphore(name))

        h = sb("h", [P, TILES, D])
        actT = sb("actT", [P, KC, max_n])
        kv_t = sb("kT", [P, KC, SEQ])
        key_sc = sb("key_sc", [P, SC_TILES * PH, 2 * K1])
        v_all = sb("v_all", [P, TILES, D])
        assert KC * max_n == PH * 2 * K1
        qT = key_sc[:, 2 * PH:3 * PH, :].rearrange("p h k -> p (h k)").rearrange("p (c n) -> p c n", c=KC)
        sk_raw = key_sc[:, PH:2 * PH, :].rearrange("p h k -> p (h k)").rearrange("p (c n) -> p c n", c=2 * PH)
        qyT = sb("qyT", [P, 3, max_n])
        w_ring = sb("w_ring", [P, W_RING, KC, SLAB])
        xs = sb("xs", [P, D])
        hn = sb("hn", [P, D])
        fin = sb("fin", [P, D])
        u_ring = sb("u_ring", [P, U_RING, D])
        v_ring = sb("v_ring", [P, V_RING, D])
        s_maps = sb("s_maps", [P, S_RING, SEQ])
        pT = sb("pT", [P, 2, SEQ])
        mix = sb("mix", [P, D])
        causal = sb("causal", [P, SEQ])
        dist = sb("dist", [P, SEQ])
        g2b = sb("g2b", [P, D])
        gfb = sb("gfb", [P, D])
        g1r = sb("g1r", [KC, P])
        g1c = sb("g1c", [P, KC])
        sub_c = sb("sub_c", [P, 1])
        subkT = sb("subkT", [P, 2 * PH, K1])
        ident = sb("ident", [P, P])
        diag = sb("diag", [P, COLS, P])
        wf = sb("wf", [P, KC, FH])
        bf = sb("bf", [FH, 1])
        c_all = sb("c_all", [FH, SEQ])
        z_f = sb("z_f", [FH, max_n])
        e_f = sb("e_f", [FH, max_n])
        selq = sb("selq", [P, FH, P])
        caug = sb("caug", [P, SEQ])
        ones = sb("ones", [P, 1])
        eps = sb("eps", [P, 1])
        ones_row = sb("ones_row", [1, P])
        lam_in = sb("lam_in", [1, 4, HD])
        lam_s = sb("lam_s", [1, 8])
        neglam = sb("neglam", [P, 1])
        stat = sb("stat", [P, 16])
        rstd2 = sb("rstd2", [P, TILES])
        negmax = sb("negmax", [P, MAPS])
        rowsum = sb("rowsum", [P, MAPS])
        rinv = sb("rinv", [P, MAPS])
        iota_i = sb("iota_i", [P, 16], I32)
        iota_f = sb("iota_f", [P, 16])
        tk_v = sb("tk_v", [P, 2, TOPK])
        tk_i = sb("tk_i", [P, 2, TOPK], U32)
        tk_if = sb("tk_if", [P, 2, TOPK])
        tk_s = sb("tk_s", [P, 2, K1])
        tk_w = sb("tk_w", [P, 2, K1])
        cand = sb("cand", [P, TOPK, TOPK])
        cand_w = sb("cand_w", [P, TOPK, TOPK])
        top_v = sb("top_v", [P, TOPK])
        top_p = sb("top_p", [P, TOPK], U32)
        top_hl = sb("top_hl", [P, 2, TOPK], U32)
        top_hlf = sb("top_hlf", [P, 2, TOPK])
        onehot = sb("onehot", [P, 2 * TOPK, TOPK])
        picked = sb("picked", [P, 2, TOPK])
        eidx = [sb(f"eidx{i}", [P, TOPK], I32) for i in range(2)]
        gneg = sb("gneg", [P, 1])
        gexp = sb("gexp", [P, TOPK])
        fin_inv = sb("fin_inv", [P, 1])
        gsum = sb("gsum", [P, 1])
        gate = sb("gate", [P, 2, TOPK])
        hid = sb("hid", [P, 2, TOPK])
        gel = sb("gel", [P, 2, TOPK])
        coef = sb("coef", [P, 2, TOPK])

        def bank(name):
            return ctx.enter_context(nc.psum_tensor(name, [P, BANK], F32))

        acc = [bank("acc0"), bank("acc1")]
        mm = [bank("mm0"), bank("mm1")]
        sc_b = [bank("sc0"), bank("sc1")]
        tr_b = bank("tr")
        o_b = bank("o")

        x_in = [sem(f"x_in{t}") for t in range(TILES)]
        consts_in = sem("consts_in")
        g1_in = sem("g1_in")
        gains_in = sem("gains_in")
        slab_in = [sem(f"slab_in{i}") for i in range(W_RING)]
        pool_const = sem("pool_const")
        dve_const = sem("dve_const")
        mm_full, mm_drained = sem("mm_full"), sem("mm_drained")
        xs_ready = sem("xs_ready")
        act_norm = sem("act_norm")
        dve_chain = sem("dve_chain")
        norm_ask = sem("norm_ask")
        selq_ready = sem("selq_ready")
        sc_full, sc_drained = sem("sc_full"), sem("sc_drained")
        exp_done = sem("exp_done")
        comb_done = sem("comb_done")
        tr_full, tr_drained = sem("tr_full"), sem("tr_drained")
        pv_done = sem("pv_done")
        o_drained = sem("o_drained")
        topk_step = sem("topk_step")
        gexp_done = sem("gexp_done")
        u_in = [sem(f"u_in{i}") for i in range(U_RING)]
        v_in = [sem(f"v_in{i}") for i in range(V_RING)]
        dot_done = sem("dot_done")
        gelu_done = sem("gelu_done")
        coef_done = sem("coef_done")
        diag_done = sem("diag_done")
        v_used = sem("v_used")
        v_added = sem("v_added")
        acc_drained = sem("acc_drained")
        fin_step = sem("fin_step")
        fin_root = sem("fin_root")
        hn_ready = sem("hn_ready")
        out_done = sem("out_done")

        GRP = TOPK // COLS

        def pieces_after(tile, head, grp):
            for g, host in HOST_TILES.items():
                if host == tile:
                    ps, slots = PIECES[g], PH * GRP - 1
                    k = head * GRP + grp
                    return weigh(ps, k, slots)
            return []

        def weigh(ps, k, slots):
            cost = {"norm1": 2, "project": 6, "forget": 2, "attend": 1.6, "mix": 3, "outproj": 5, "norm2": 3, "query": 7}
            n = {0: 1, 1: 1, 2: 2}
            total = sum(cost[p[0]] for p in ps)
            at, picked_now = 0.0, []
            for p in ps:
                at += cost[p[0]]
                if min(slots - 1, int((at - 1e-6) / total * slots)) == k:
                    picked_now.append(p)
            return picked_now

        def tile_of(n):
            return n // PH if isinstance(n, int) else TILES - 1

        def counted(n, c, vector):
            def per_step(tile):
                return V_ON_VECTOR[tile] if vector else COLS - V_ON_VECTOR[tile]

            if isinstance(n, int) and c < 0:
                if n == 0:
                    return 0
                n, c = n - 1, c + TOPK
            tile = tile_of(n)
            lead = V_ON_VECTOR[tile]
            step, within = c // COLS, c % COLS + 1
            within = min(within, lead) if vector else max(0, within - lead)
            if isinstance(n, int):
                before = sum(per_step(m // PH) for m in range(n)) * GRP
                return before + per_step(tile) * step + within
            n0 = PH * len(HOST_TILES)
            before = sum(per_step(m // PH) for m in range(n0)) * GRP
            if per_step(tile) == 0:
                return before
            return before - GRP * per_step(tile) * n0 + GRP * per_step(tile) * n + per_step(tile) * step + within

        def on_tensor(n, c):
            return counted(n, c, False)

        def on_vector(n, c):
            return counted(n, c, True)

        assert len(set(V_ON_VECTOR[len(HOST_TILES):])) == 1 and V_ON_VECTOR[-1] == 0 and V_RING == COLS

        TK = 29
        TK_IDX = 26
        TK_NEG = 27
        FIN = 3

        block = ctx.enter_context(nc.Block())

        @block.sync
        def _(sp):
            sp.dma_start(h[:, 0, :], x[0, 0:P, :]).then_inc(x_in[0], 16)
            sp.dma_start(g1r[:, :], norm1_g[0].rearrange("(c p) -> c p", p=P)).then_inc(g1_in, 16)
            sp.dma_start(sk_raw, peer_sub_keys[0].rearrange("h s k d -> k (h s) d")).then_inc(consts_in, 16)
            for i, v in enumerate((lambda_q1, lambda_q2, lambda_k1, lambda_k2)):
                sp.dma_start(lam_in[:, i, :], v).then_inc(consts_in, 16)
            sp.dma_start(sub_c[:, :], subln_g.rearrange("a p -> p a")).then_inc(consts_in, 16)
            sp.dma_start(wf[:, :, :], w_in[0][:, 3 * FW:3 * FW + FH].rearrange("(c p) n -> p c n", p=P)).then_inc(consts_in, 16)
            sp.dma_start(bf[:, :], b_f.rearrange("a p -> p a")).then_inc(consts_in, 16)

            def load_slab(n):
                if n >= W_RING:
                    sp.wait_ge(mm_full, slab_last_use[n - W_RING] + 1)
                sp.dma_start(w_ring[:, n % W_RING, :, :],
                             slab_src[n % SLABS].rearrange("(c p) n -> p c n", p=P)).then_inc(slab_in[n % W_RING], 16)

            for n in range(W_RING):
                load_slab(n)
            sp.dma_start(g2b[:, :], norm2_g.broadcast_to([P, D])).then_inc(gains_in, 16)
            sp.dma_start(gfb[:, :], final_g.rearrange("(a n) -> a n", a=1).broadcast_to([P, D])).then_inc(gains_in, 16)
            for t in range(1, TILES):
                sp.dma_start(h[:, t, :], x[0, t * P:(t + 1) * P, :]).then_inc(x_in[t], 16)
            for n in range(W_RING, len(GROUPS) * SLABS):
                load_slab(n)

            with sp.Fori(0, TILES) as t:
                sp.wait_ge(fin_step, FIN * t + FIN)
                sp.dma_start(out[0, bass.ds(t * P, P), :], fin[:, :]).then_inc(out_done, 16)
            sp.wait_ge(out_done, 16 * TILES)

        @block.gpsimd
        def _(pool):
            nc.gpsimd.memset(ident[:, :], 0.0).then_inc(pool_const, 1)
            nc.gpsimd.memset(causal[:, :], 0.0).then_inc(pool_const, 1)
            nc.gpsimd.iota(fin[:, 0:SEQ].bitcast(I32), pattern=[[1, SEQ]], base=-(SEQ - P), channel_multiplier=-1).then_inc(pool_const, 1)
            nc.gpsimd.iota(iota_i[:, :], pattern=[[1, TOPK]], base=0, channel_multiplier=0).then_inc(pool_const, 1)
            pool.wait_ge(pool_const, 4)
            nc.gpsimd.affine_select(out=ident[:, :], in_=ident[:, :], compare_op=ALU.not_equal, fill=1.0,
                                    base=0, pattern=[[-1, P]], channel_multiplier=1).then_inc(pool_const, 1)
            nc.gpsimd.affine_select(out=causal[:, SEQ - P:SEQ], in_=causal[:, SEQ - P:SEQ], compare_op=ALU.is_ge, fill=-BIG,
                                    base=0, pattern=[[-1, P]], channel_multiplier=1).then_inc(pool_const, 1)

            def gathers(n, par, first):
                pool.wait_ge(topk_step, TK * n + TK_IDX)
                pool.nop(nofuse=True)
                for g0 in range(0, TOPK, COLS):
                    for c in range(g0, g0 + COLS):
                        if not (first and c < U_RING):
                            pool.wait_ge(dot_done, TOPK * n + c + 1 - U_RING)
                            pool.nop(nofuse=True)
                        nc.gpsimd.indirect_dma_start(
                            out=u_ring[:, c % U_RING, :], out_offset=None, in_=peer_u[0],
                            in_offset=bass.IndirectOffsetOnAxis(ap=eidx[par][:, c:c + 1], axis=0)).then_inc(u_in[c % U_RING], 16)
                    for c in range(g0, g0 + COLS):
                        if not (first and c < V_RING):
                            pool.wait_ge(v_used, on_tensor(n, c - V_RING))
                            pool.nop(nofuse=True)
                            if on_vector(n, c - V_RING):
                                pool.wait_ge(v_added, on_vector(n, c - V_RING))
                                pool.nop(nofuse=True)
                        nc.gpsimd.indirect_dma_start(
                            out=v_ring[:, c % V_RING, :], out_offset=None, in_=peer_v[0],
                            in_offset=bass.IndirectOffsetOnAxis(ap=eidx[par][:, c:c + 1], axis=0)).then_inc(v_in[c % V_RING], 16)

            for n in range(PH * len(HOST_TILES)):
                gathers(n, n % 2, n == 0)
            with pool.Fori(PH * len(HOST_TILES) // 2, HEADS // 2) as i:
                for par in range(2):
                    gathers(2 * i + par, par, False)

        @block.tensor
        def _(pe):
            def mm_bank(name):
                n = mm_no[name]
                if n >= 2:
                    pe.wait_ge(mm_drained, n - 1)
                return mm[n % 2]

            def transposes(name, src):
                b = mm_bank(name)
                for j in range(4):
                    last = nc.tensor.transpose(b[:, j * P:(j + 1) * P], src(j), ident[:, :])
                last.then_inc(mm_full, 1)

            def slab(g, s):
                n = g * SLABS + s
                pe.wait_ge(slab_in[n % W_RING], 16 * (n // W_RING + 1))
                return w_ring[:, n % W_RING, :, :]

            def piece(kind, a, b):
                if kind == "norm1":
                    pe.wait_ge(xs_ready, xs_no[("norm1", b)])
                    for hf in range(2):
                        transposes(("xT", b, hf), lambda j: xs[:, (4 * hf + j) * P:(4 * hf + j + 1) * P])
                elif kind == "project":
                    g, n = a, P * len(GROUPS[a])
                    w = slab(g, b)
                    pe.wait_ge(mm_drained, mm_done(("xT", GROUPS[g][-1], 1)))
                    if in_kinds[b][0] in ("va", "vb"):
                        for j, t in enumerate(GROUPS[g]):
                            bk = mm_bank(("v", b, t))
                            for c in range(KC):
                                last = nc.tensor.matmul(bk[:, 0:SLAB], actT[:, c, j * P:(j + 1) * P], w[:, c, :],
                                                        start=(c == 0), stop=(c == KC - 1))
                            last.then_inc(mm_full, 1)
                    else:
                        for q in range(2):
                            bk = mm_bank(("qk", g, b, q))
                            for c in range(KC):
                                last = nc.tensor.matmul(bk[:, 0:n], w[:, c, q * P:(q + 1) * P], actT[:, c, 0:n],
                                                        start=(c == 0), stop=(c == KC - 1))
                            last.then_inc(mm_full, 1)
                elif kind == "forget":
                    n = P * len(GROUPS[a])
                    pe.wait_ge(consts_in, 16 * 8)
                    bk = mm_bank(("forget", a))
                    for c in range(KC):
                        last = nc.tensor.matmul(bk[0:FH, 0:n], wf[:, c, :], actT[:, c, 0:n], start=(c == 0), stop=(c == KC - 1))
                    last.then_inc(mm_full, 1)
                elif kind == "lambda":
                    pe.wait_ge(dve_const, 1)
                    nc.tensor.matmul(mm_bank(("lambda",))[:, 0:1], ones_row[:, :], lam_s[0:1, 4:5],
                                     start=True, stop=True).then_inc(mm_full, 1)
                elif kind == "subkeys":
                    for i in range(2 * PH // 4):
                        transposes(("subkeys", i), lambda j: sk_raw[:, 4 * i + j, :])
                elif kind == "attend":
                    attend(a, b)
                elif kind == "mix":
                    for hf in range(2):
                        if hf == 0:
                            pe.wait_ge(o_drained, 2 * b + 1)
                        else:
                            pe.wait_ge(xs_ready, xs_no[("mix", b)])
                        transposes(("mixT", b, hf), lambda j: mix[:, (4 * hf + j) * P:(4 * hf + j + 1) * P])
                elif kind == "outproj":
                    w = slab(a, N_IN + b)
                    for j, t in enumerate(GROUPS[a]):
                        pe.wait_ge(mm_drained, mm_done(("mixT", t, 1)))
                        bk = mm_bank(("out", b, t))
                        for c in range(KC):
                            last = nc.tensor.matmul(bk[:, 0:SLAB], actT[:, c, j * P:(j + 1) * P], w[:, c, :],
                                                    start=(c == 0), stop=(c == KC - 1))
                        last.then_inc(mm_full, 1)
                elif kind == "norm2":
                    pe.wait_ge(xs_ready, xs_no[("norm2", b)])
                    for hf in range(2):
                        transposes(("hT", b, hf), lambda j: xs[:, (4 * hf + j) * P:(4 * hf + j + 1) * P])
                elif kind == "query":
                    g, n = a, P * len(GROUPS[a])
                    pe.wait_ge(mm_drained, mm_done(("hT", GROUPS[g][-1], 1)))

                    def query_chunk(c2, w):
                        bk = mm_bank(("query", g, c2))
                        for c in range(KC):
                            last = nc.tensor.matmul(bk[:, 0:n], w[:, c, (c2 % 2) * P:(c2 % 2 + 1) * P], actT[:, c, 0:n],
                                                    start=(c == 0), stop=(c == KC - 1))
                        last.then_inc(mm_full, 1)

                    if b < PH:
                        w = slab(g, N_IN + N_OUT + b)
                        query_chunk(2 * b, w)
                    if b > 0:
                        pe.wait_ge(mm_drained, mm_done(("query", g, 2 * b - 1)))
                        for j, t in enumerate(GROUPS[g]):
                            bk = mm_bank(("keys", b - 1, t))
                            for s in range(2):
                                c2 = 2 * (b - 1) + s
                                last = nc.tensor.matmul(bk[:, s * K1:(s + 1) * K1], qyT[:, c2 % 3, j * P:(j + 1) * P], subkT[:, c2, :],
                                                        start=True, stop=True)
                            last.then_inc(mm_full, 1)
                    if b < PH:
                        query_chunk(2 * b + 1, w)

            def attend(t, step):
                nk = P * (t + 1)
                g = next(i for i, ts in enumerate(GROUPS) if t in ts)
                j = GROUPS[g].index(t)
                if step == 0:
                    pe.wait_ge(mm_drained, mm_done(("v", N_IN - 1, GROUPS[g][-1])))
                    pe.wait_ge(selq_ready, 2 * (t + 1))
                if step < ITEMS:
                    for m in maps_of(step):
                        k = MAPS * t + m
                        if k >= 2:
                            pe.wait_ge(sc_drained, k - 1)
                        bk = sc_b[k % 2]
                        if m < FH:
                            lo, ch = HD * (m % 2), m // 2
                        else:
                            lo, ch = HD * ((m - FH) % 2), KC // 2 + (m - FH) // 2
                        mo = nc.tensor.matmul(bk[:, 0:nk], qT[lo:lo + HD, ch, j * P:(j + 1) * P], kv_t[lo:lo + HD, ch, 0:nk],
                                              start=True, stop=(m >= FH))
                        if m < FH:
                            mo = nc.tensor.matmul(bk[:, 0:nk], selq[lo:lo + 40, m, :], caug[lo:lo + 40, 0:nk], start=False, stop=True)
                        mo.then_inc(sc_full, 1)
                it = step - 2
                if 0 <= it < ITEMS:
                    k = ITEMS * t + it
                    if it < FH:
                        pe.wait_ge(exp_done, MAPS * t + it + 1)
                    else:
                        pe.wait_ge(comb_done, NDH * t + it - FH + 1)
                    if k >= 1:
                        pe.wait_ge(tr_drained, k)
                    slot = (MAPS * t + maps_of(it)[0]) % S_RING
                    for q in range(t + 1):
                        last = nc.tensor.transpose(tr_b[:, q * P:(q + 1) * P], s_maps[:, slot, q * P:(q + 1) * P], ident[:, :])
                    last.then_inc(tr_full, 1)
                it = step - 3
                if 0 <= it < ITEMS:
                    k = ITEMS * t + it
                    pe.wait_ge(tr_drained, k + 1)
                    if it == 0 and t > 0:
                        pe.wait_ge(o_drained, 2 * t)
                    if it == FH:
                        pe.wait_ge(o_drained, 2 * t + 1)
                    w = HD if it < FH else DH
                    col = HD * it if it < FH else DH * (it - FH)
                    vcol = col if it < FH else FW + col
                    for q in range(t + 1):
                        last = nc.tensor.matmul(o_b[:, col:col + w], pT[:, k % 2, q * P:(q + 1) * P], v_all[:, q, vcol:vcol + w],
                                                start=(q == 0), stop=(q == t))
                    last.then_inc(pv_done, 1)

            def peer_group(n, g0, starts, emptied):
                first = V_ON_VECTOR[tile_of(n)]
                for c in range(g0 + first, g0 + COLS):
                    if c == first and emptied is not None:
                        pe.wait_ge(acc_drained, emptied)
                    pe.wait_ge(v_in[c % V_RING], 16 * (TOPK // V_RING) * n + 16 * (c // V_RING + 1))
                    pe.wait_ge(diag_done, on_tensor(n, c))
                    for half in range(2):
                        last = nc.tensor.matmul(acc[half][:, :], diag[:, c % COLS, :], v_ring[:, c % V_RING, half * BANK:(half + 1) * BANK],
                                                start=(starts and c == first), stop=False, skip_group_check=True)
                    last.then_inc(v_used, 1)

            pe.wait_ge(pool_const, 6)
            pe.wait_ge(g1_in, 16)
            nc.tensor.transpose(mm_bank(("gain1",))[:, 0:KC], g1r[:, :], ident[0:KC, 0:KC]).then_inc(mm_full, 1)
            for p_ in PIECES[0]:
                piece(*p_)
            for tile in sorted(HOST_TILES.values()):
                for head in range(PH):
                    for grp in range(GRP):
                        for p_ in pieces_after(tile, head, grp):
                            piece(*p_)
                        peer_group(PH * tile + head, grp * COLS, head == 0, 2 * tile if tile and head == 0 else None)
            with pe.Fori(len(HOST_TILES), TILES) as t:
                for par in range(2):
                    for grp in range(GRP):
                        peer_group(PH * t + par, grp * COLS, par == 0, 2 * t if par == 0 else None)
                with pe.Fori(1, PH // 2) as i:
                    for par in range(2):
                        for grp in range(GRP):
                            peer_group(PH * t + 2 * i + par, grp * COLS, False, None)

        @block.scalar
        def _(act):
            asked = [0]
            given = [0]

            def root(dst, src, scale, count=None):
                asked[0] += 1
                given[0] += 1
                act.wait_ge(norm_ask, asked[0])
                nc.scalar.activation(dst, src, ACT.Sqrt, scale=scale, bias=eps[:, 0:1]).then_inc(act_norm, 1)

            def piece(kind, a, b):
                if kind == "norm1":
                    root(stat[:, 1:2], stat[:, 0:1], 1.0 / D)
                elif kind == "norm2":
                    root(stat[:, 5:6], stat[:, 4:5], 1.0 / D)
                elif kind == "mix":
                    root(stat[:, 12:12 + NDH], stat[:, 8:8 + NDH], 1.0 / DH)
                elif kind == "lambda":
                    asked[0] += 1
                    given[0] += 1
                    act.wait_ge(norm_ask, asked[0])
                    nc.scalar.activation(lam_s[0:1, 2:4], lam_s[0:1, 0:2], ACT.Exp).then_inc(act_norm, 1)
                elif kind == "forget":
                    n = P * len(GROUPS[a])
                    asked[0] += 1
                    act.wait_ge(norm_ask, asked[0])
                    nc.scalar.activation(e_f[:, 0:n], e_f[:, 0:n], ACT.Exp, scale=-1.0).then_inc(act_norm, 1)
                    given[0] += 2
                    act.wait_ge(act_norm, given[0] - 1)
                    nc.scalar.activation(e_f[:, 0:n], e_f[:, 0:n], ACT.Ln, bias=1.0).then_inc(act_norm, 1)
                elif kind == "attend":
                    t, step = a, b
                    nk = P * (t + 1)
                    if step < ITEMS:
                        for m in maps_of(step):
                            k = MAPS * t + m
                            act.wait_ge(sc_drained, k + 1)
                            s = s_maps[:, k % S_RING, 0:nk]
                            nc.scalar.activation(s, s, ACT.Exp, scale=-1.0, bias=negmax[:, m:m + 1],
                                                 accum_out=rowsum[:, m:m + 1]).then_inc(exp_done, 1)
                    it = step - 2
                    if 0 <= it < ITEMS:
                        k = ITEMS * t + it
                        act.wait_ge(tr_full, k + 1)
                        if k >= 2:
                            act.wait_ge(pv_done, k - 1)
                        nc.scalar.activation(pT[:, k % 2, 0:nk], tr_b[:, 0:nk], ACT.Copy).then_inc(tr_drained, 1)

            def gate_exp(n):
                act.wait_ge(topk_step, TK * n + TK_NEG)
                nc.scalar.activation(gexp[:, :], top_v[:, :], ACT.Exp, bias=gneg[:, 0:1], accum_out=gsum[:, 0:1]).then_inc(gexp_done, 1)

            def peer_group(n, par, g0, first):
                act.wait_ge(dot_done, TOPK * n + g0 + COLS)
                nc.scalar.activation(gel[:, par, g0:g0 + COLS], hid[:, par, g0:g0 + COLS], ACT.Gelu).then_inc(gelu_done, 1)
                act.wait_ge(coef_done, GRP * n + g0 // COLS + 1)
                for c in range(V_ON_VECTOR[tile_of(n)], COLS):
                    if not (first and g0 == 0):
                        act.wait_ge(v_used, on_tensor(n, g0 + c - COLS))
                    nc.scalar.activation(diag[:, c, :], ident[:, :], ACT.Copy,
                                         scale=coef[:, par, g0 + c:g0 + c + 1]).then_inc(diag_done, 1)

            def fin_rt(t):
                act.wait_ge(fin_step, FIN * t + 1)
                nc.scalar.activation(stat[:, 7:8], stat[:, 6:7], ACT.Sqrt, scale=1.0 / D, bias=eps[:, 0:1]).then_inc(fin_root, 1)

            act.wait_ge(pool_const, 6)
            for p_ in PIECES[0]:
                piece(*p_)
            gate_exp(0)
            for tile in sorted(HOST_TILES.values()):
                for head in range(PH):
                    for grp in range(GRP):
                        peer_group(PH * tile + head, head % 2, grp * COLS, tile == 0 and head == 0)
                        if tile and head == 0 and grp == 0:
                            fin_rt(tile - 1)
                        if grp == 1 and not (head == PH - 1):
                            gate_exp(PH * tile + head + 1)
                        for p_ in pieces_after(tile, head, grp):
                            piece(*p_)
                        if grp == GRP - 1 and head == PH - 1:
                            gate_exp(PH * tile + head + 1)
            rest = len(HOST_TILES)
            with act.Fori(rest, TILES) as t:
                for par in range(2):
                    for grp in range(GRP):
                        peer_group(PH * t + par, par, grp * COLS, False)
                        if par == 0 and grp == 0:
                            fin_rt(t - 1)
                        if grp == 1:
                            gate_exp(PH * t + par + 1)
                with act.Fori(1, PH // 2) as i:
                    for par in range(2):
                        for grp in range(GRP):
                            peer_group(PH * t + 2 * i + par, par, grp * COLS, False)
                            if grp == 1:
                                gate_exp(PH * t + 2 * i + par + 1)
            fin_rt(TILES - 1)

        @block.vector
        def _(dve):
            chain = [0]
            rooted = [0]
            handed = [0]

            def link(ins):
                chain[0] += 1
                ins.then_inc(dve_chain, 1)
                dve.wait_ge(dve_chain, chain[0])

            def from_act(ins, steps=1):
                ins.then_inc(norm_ask, 1)
                rooted[0] += steps
                dve.wait_ge(act_norm, rooted[0])

            def mm_wait(name):
                dve.wait_ge(mm_full, mm_done(name))
                return mm[mm_no[name] % 2]

            def four(b):
                return b[:, :].rearrange("p (c n) -> p c n", c=4)

            def norm_rows(src, st, width_scale=None):
                from_act(nc.vector.tensor_tensor_reduce(out=xs[:, :], in0=src, in1=src, scale=1.0, scalar=0.0,
                                                        op0=ALU.mult, op1=ALU.add, accum_out=stat[:, st:st + 1]))

            def piece(kind, a, b):
                if kind == "norm1":
                    g, t = a, b
                    j = GROUPS[g].index(t)
                    dve.wait_ge(x_in[t], 16)
                    if xs_prev[("norm1", t)] is not None:
                        dve.wait_ge(mm_full, mm_done(xs_prev[("norm1", t)]))
                    norm_rows(h[:, t, :], 0)
                    link(nc.vector.reciprocal(stat[:, 2:3], stat[:, 1:2]))
                    nc.vector.tensor_scalar(xs[:, :], h[:, t, :], stat[:, 2:3], None, ALU.mult).then_inc(xs_ready, 1)
                    if j == 0 and g > 0:
                        dve.wait_ge(mm_full, mm_done(("query", g - 1, 2 * PH - 1)))
                    for hf in range(2):
                        bk = mm_wait(("xT", t, hf))
                        nc.vector.tensor_tensor(out=actT[:, 4 * hf:4 * hf + 4, j * P:(j + 1) * P], in0=four(bk),
                                                in1=g1c[:, 4 * hf:4 * hf + 4].unsqueeze(2).broadcast_to([P, 4, P]),
                                                op=ALU.mult).then_inc(mm_drained, 1)
                elif kind == "project":
                    g, s = a, b
                    n = P * len(GROUPS[g])
                    knd, _, col = in_kinds[s]
                    if knd in ("va", "vb"):
                        col += FW if knd == "vb" else 0
                        for t in GROUPS[g]:
                            bk = mm_wait(("v", s, t))
                            nc.vector.tensor_copy(v_all[:, t, col:col + SLAB], bk[:, 0:SLAB]).then_inc(mm_drained, 1)
                    else:
                        for q in range(2):
                            ch = col // P + q + (KC // 2 if knd in ("qb", "kb") else 0)
                            bk = mm_wait(("qk", g, s, q))
                            if knd in ("ka", "kb"):
                                t0 = GROUPS[g][0] * P
                                nc.vector.tensor_copy(kv_t[:, ch, t0:t0 + n], bk[:, 0:n]).then_inc(mm_drained, 1)
                            else:
                                f = HD ** -0.5 if knd == "qa" else -(HD ** -0.5) / slopes[ch - KC // 2]
                                nc.vector.tensor_scalar(qT[:, ch, 0:n], bk[:, 0:n], f, None, ALU.mult).then_inc(mm_drained, 1)
                elif kind == "forget":
                    g = a
                    n, t0 = P * len(GROUPS[g]), P * GROUPS[g][0]
                    dve.wait_ge(consts_in, 16 * 8)
                    bk = mm_wait(("forget", g))
                    nc.vector.tensor_scalar(z_f[:, 0:n], bk[0:FH, 0:n], bf[:, 0:1], None, ALU.add).then_inc(mm_drained, 1)
                    dve.wait_ge(mm_drained, mm_done(("forget", g)))
                    from_act(nc.vector.scalar_tensor_tensor(out=e_f[:, 0:n], in0=z_f[:, 0:n], scalar=-1.0, in1=z_f[:, 0:n],
                                                            op0=ALU.mult, op1=ALU.max), 2)
                    link(nc.vector.scalar_tensor_tensor(out=z_f[:, 0:n], in0=z_f[:, 0:n], scalar=0.0, in1=e_f[:, 0:n],
                                                        op0=ALU.min, op1=ALU.subtract))
                    init = 0.0 if t0 == 0 else c_all[:, t0 - 1:t0]
                    link(nc.vector.tensor_tensor_scan(c_all[:, t0:t0 + n], ones[0:FH, :].broadcast_to([FH, n]), z_f[:, 0:n],
                                                      init, ALU.mult, ALU.add))
                    for lo in (0, HD):
                        link(nc.vector.tensor_scalar(caug[lo:lo + FH, t0:t0 + n], c_all[:, t0:t0 + n], -1.0, None, ALU.mult))
                elif kind == "lambda":
                    link(nc.vector.tensor_tensor(out=lam_in[:, 0:2, :], in0=lam_in[:, 0:2, :], in1=lam_in[:, 2:4, :], op=ALU.mult))
                    from_act(nc.vector.tensor_reduce(lam_s[0:1, 0:2], lam_in[:, 0:2, :], AX, ALU.add))
                    link(nc.vector.tensor_tensor(out=lam_s[0:1, 5:6], in0=lam_s[0:1, 3:4], in1=lam_s[0:1, 2:3], op=ALU.subtract))
                    nc.vector.tensor_scalar(lam_s[0:1, 4:5], lam_s[0:1, 5:6], LAMBDA_INIT, None, ALU.subtract).then_inc(dve_const, 1)
                    bk = mm_wait(("lambda",))
                    nc.vector.tensor_copy(neglam[:, :], bk[:, 0:1]).then_inc(mm_drained, 1)
                    dve.wait_ge(mm_drained, mm_done(("lambda",)))
                elif kind == "subkeys":
                    for i in range(2 * PH // 4):
                        bk = mm_wait(("subkeys", i))
                        nc.vector.tensor_copy(subkT[:, 4 * i:4 * i + 4, :], four(bk)).then_inc(mm_drained, 1)
                elif kind == "attend":
                    attend(a, b)
                elif kind == "mix":
                    g, t = a, b
                    j = GROUPS[g].index(t)
                    dve.wait_ge(pv_done, ITEMS * (t + 1))
                    nc.vector.tensor_copy(mix[:, FW:D], o_b[:, :]).then_inc(o_drained, 1)
                    dve.wait_ge(o_drained, 2 * t + 2)
                    if xs_prev[("mix", t)] is not None:
                        dve.wait_ge(mm_full, mm_done(xs_prev[("mix", t)]))
                    link(nc.vector.tensor_tensor(out=xs[:, 0:FW], in0=mix[:, FW:D], in1=mix[:, FW:D], op=ALU.mult))
                    from_act(nc.vector.tensor_reduce(stat[:, 8:8 + NDH], xs[:, 0:FW].rearrange("p (a n) -> p a n", a=NDH),
                                                     AX, ALU.add))
                    link(nc.vector.reciprocal(rinv[:, 0:NDH], stat[:, 12:12 + NDH]))
                    mb = mix[:, FW:D].rearrange("p (a n) -> p a n", a=NDH)
                    nc.vector.tensor_tensor(out=mb, in0=mb, in1=rinv[:, 0:NDH].unsqueeze(2).broadcast_to([P, NDH, DH]),
                                            op=ALU.mult).then_inc(xs_ready, 1)
                    bk = mm_wait(("mixT", t, 0))
                    nc.vector.tensor_copy(actT[:, 0:4, j * P:(j + 1) * P], four(bk)).then_inc(mm_drained, 1)
                    bk = mm_wait(("mixT", t, 1))
                    nc.vector.tensor_scalar(actT[:, 4:8, j * P:(j + 1) * P], four(bk), sub_c[:, 0:1], 1.0 - LAMBDA_INIT,
                                            ALU.mult, ALU.mult).then_inc(mm_drained, 1)
                elif kind == "outproj":
                    for t in GROUPS[a]:
                        bk = mm_wait(("out", b, t))
                        hs = h[:, t, b * SLAB:(b + 1) * SLAB]
                        nc.vector.tensor_tensor(out=hs, in0=bk[:, 0:SLAB], in1=hs, op=ALU.add).then_inc(mm_drained, 1)
                elif kind == "norm2":
                    g, t = a, b
                    j = GROUPS[g].index(t)
                    dve.wait_ge(mm_drained, mm_done(("out", N_OUT - 1, t)))
                    dve.wait_ge(mm_full, mm_done(xs_prev[("norm2", t)]))
                    norm_rows(h[:, t, :], 4)
                    if t == 0:
                        dve.wait_ge(gains_in, 16 * 2)
                    link(nc.vector.reciprocal(rstd2[:, t:t + 1], stat[:, 5:6]))
                    nc.vector.scalar_tensor_tensor(out=xs[:, :], in0=h[:, t, :], scalar=rstd2[:, t:t + 1], in1=g2b[:, :],
                                                   op0=ALU.mult, op1=ALU.mult).then_inc(xs_ready, 1)
                    for hf in range(2):
                        bk = mm_wait(("hT", t, hf))
                        nc.vector.tensor_copy(actT[:, 4 * hf:4 * hf + 4, j * P:(j + 1) * P], four(bk)).then_inc(mm_drained, 1)
                elif kind == "query":
                    g, n = a, P * len(GROUPS[a])

                    def query_out(c2):
                        bk = mm_wait(("query", g, c2))
                        nc.vector.tensor_copy(qyT[:, c2 % 3, 0:n], bk[:, 0:n]).then_inc(mm_drained, 1)

                    if b < PH:
                        query_out(2 * b)
                    if b > 0:
                        for t in GROUPS[g]:
                            bk = mm_wait(("keys", b - 1, t))
                            nc.vector.tensor_copy(key_sc[:, (t % SC_TILES) * PH + b - 1, :], bk[:, 0:2 * K1]).then_inc(mm_drained, 1)
                    if b < PH:
                        query_out(2 * b + 1)

            def attend(t, step):
                nk = P * (t + 1)
                if step == 0:
                    if t > 0:
                        dve.wait_ge(sc_full, MAPS * t)
                    for lo in (0, HD):
                        nc.vector.tensor_tensor(out=selq[lo + 32:lo + 32 + FH, :, :],
                                                in0=c_all[:, t * P:(t + 1) * P].unsqueeze(1).broadcast_to([FH, FH, P]),
                                                in1=ident[0:FH, 0:FH].unsqueeze(2).broadcast_to([FH, FH, P]),
                                                op=ALU.mult).then_inc(selq_ready, 1)
                if step < ITEMS:
                    for m in maps_of(step):
                        k = MAPS * t + m
                        dve.wait_ge(sc_full, k + 1)
                        if k >= S_RING:
                            k0 = k - S_RING
                            dve.wait_ge(tr_full, ITEMS * (k0 // MAPS) + item_of(k0 % MAPS) + 1)
                        strip, scale = (causal, -1.0) if m < FH else (dist, slopes[(m - FH) // 2])
                        nc.vector.tensor_tensor_reduce(out=s_maps[:, k % S_RING, 0:nk], in0=sc_b[k % 2][:, 0:nk],
                                                       in1=strip[:, SEQ - nk:SEQ], scale=scale, scalar=HUGE,
                                                       op0=ALU.add, op1=ALU.min, accum_out=negmax[:, m:m + 1]).then_inc(sc_drained, 1)
                it = step - 1
                if FH <= it < ITEMS:
                    m1, m2 = maps_of(it)
                    dve.wait_ge(exp_done, MAPS * t + m2 + 1)
                    link(nc.vector.reciprocal(rinv[:, m1:m2 + 1], rowsum[:, m1:m2 + 1]))
                    link(nc.vector.tensor_scalar(rinv[:, m2:m2 + 1], rinv[:, m2:m2 + 1], neglam[:, 0:1], None, ALU.mult))
                    s1 = s_maps[:, (MAPS * t + m1) % S_RING, 0:nk]
                    s2 = s_maps[:, (MAPS * t + m2) % S_RING, 0:nk]
                    link(nc.vector.tensor_scalar(s2, s2, rinv[:, m2:m2 + 1], None, ALU.mult))
                    nc.vector.scalar_tensor_tensor(out=s1, in0=s1, scalar=rinv[:, m1:m1 + 1], in1=s2,
                                                   op0=ALU.mult, op1=ALU.add).then_inc(comb_done, 1)
                if step == FH + 2:
                    dve.wait_ge(pv_done, ITEMS * t + FH)
                    link(nc.vector.reciprocal(rinv[:, 0:FH], rowsum[:, 0:FH]))
                    if t > 0:
                        dve.wait_ge(mm_full, mm_done(("mixT", t - 1, 1)))
                    nc.vector.tensor_tensor(out=mix[:, 0:FW].rearrange("p (a n) -> p a n", a=FH),
                                            in0=o_b[:, :].rearrange("p (a n) -> p a n", a=FH),
                                            in1=rinv[:, 0:FH].unsqueeze(2).broadcast_to([P, FH, HD]),
                                            op=ALU.mult).then_inc(o_drained, 1)

            def after_topk(n, k):
                dve.wait_ge(topk_step, TK * n + k)
                dve.nop(nofuse=True)

            def topk_first(n, par):
                def after(k):
                    after_topk(n, k)

                s = key_sc[:, n % (SC_TILES * PH), :] if isinstance(n, int) else key_sc[:, bass.ds(n % (SC_TILES * PH), 1), :].rearrange("p a k -> p (a k)")
                nc.vector.tensor_copy(tk_s[:, :, :].rearrange("p a k -> p (a k)"), s).then_inc(topk_step, 1)
                after(1)
                s1 = [tk_s[:, 0, :], tk_s[:, 1, :]]
                for q in range(2):
                    nc.vector.max(tk_v[:, q, 0:8], s1[q]).then_inc(topk_step, 1)
                for q in range(2):
                    after(q + 2)
                    nc.vector.match_replace(tk_w[:, q, :], tk_v[:, q, 0:8], s1[q], -HUGE).then_inc(topk_step, 1)
                for q in range(2):
                    nc.vector.max_index(tk_i[:, q, 0:8], tk_v[:, q, 0:8], s1[q]).then_inc(topk_step, 1)
                for q in range(2):
                    after(q + 4)
                    nc.vector.max(tk_v[:, q, 8:16], tk_w[:, q, :]).then_inc(topk_step, 1)
                for q in range(2):
                    after(q + 8)
                    nc.vector.max_index(tk_i[:, q, 8:16], tk_v[:, q, 8:16], tk_w[:, q, :]).then_inc(topk_step, 1)
                nc.vector.tensor_tensor(out=cand[:, :, :], in0=tk_v[:, 0, :].unsqueeze(2).broadcast_to([P, TOPK, TOPK]),
                                        in1=tk_v[:, 1, :].unsqueeze(1).broadcast_to([P, TOPK, TOPK]),
                                        op=ALU.add).then_inc(topk_step, 1)
                after(11)
                nc.vector.tensor_copy(tk_if[:, :, :], tk_i[:, :, :]).then_inc(topk_step, 1)

            def topk_second(n, par):
                def after(k):
                    after_topk(n, k)

                cf = cand[:, :, :].rearrange("p a b -> p (a b)")
                wf_ = cand_w[:, :, :].rearrange("p a b -> p (a b)")
                after(12)
                nc.vector.max(top_v[:, 0:8], cf).then_inc(topk_step, 1)
                after(14)
                nc.vector.match_replace(wf_, top_v[:, 0:8], cf, -HUGE).then_inc(topk_step, 1)
                nc.vector.max_index(top_p[:, 0:8], top_v[:, 0:8], cf).then_inc(topk_step, 1)
                after(15)
                nc.vector.max(top_v[:, 8:16], wf_).then_inc(topk_step, 1)
                after(17)
                nc.vector.max_index(top_p[:, 8:16], top_v[:, 8:16], wf_).then_inc(topk_step, 1)
                after(18)
                nc.vector.tensor_scalar(top_hl[:, 0, :], top_p[:, :], 4, None, ALU.logical_shift_right).then_inc(topk_step, 1)
                nc.vector.tensor_scalar(top_hl[:, 1, :], top_p[:, :], 15, None, ALU.bitwise_and).then_inc(topk_step, 1)
                after(20)
                nc.vector.tensor_copy(top_hlf[:, :, :], top_hl[:, :, :]).then_inc(topk_step, 1)
                after(21)
                nc.vector.tensor_tensor(out=onehot[:, :, :], in0=top_hlf[:, :, :].rearrange("p a b -> p (a b)").unsqueeze(2).broadcast_to([P, 2 * TOPK, TOPK]),
                                        in1=iota_f[:, :].unsqueeze(1).broadcast_to([P, 2 * TOPK, TOPK]),
                                        op=ALU.is_equal).then_inc(topk_step, 1)
                for q in range(2):
                    after(22)
                    oh = onehot[:, q * TOPK:(q + 1) * TOPK, :]
                    nc.vector.tensor_tensor(out=oh, in0=oh, in1=tk_if[:, q, :].unsqueeze(1).broadcast_to([P, TOPK, TOPK]),
                                            op=ALU.mult).then_inc(topk_step, 1)
                after(24)
                nc.vector.tensor_reduce(picked[:, :, :].rearrange("p a b -> p (a b)"), onehot[:, :, :], AX, ALU.add).then_inc(topk_step, 1)
                after(25)
                if not (isinstance(n, int) and n < 2):
                    dve.wait_ge(v_used, on_tensor(n, -1 - TOPK) if not isinstance(n, int) else on_tensor(n - 2, TOPK - 1))
                nc.vector.scalar_tensor_tensor(out=eidx[par][:, :], in0=picked[:, 0, :], scalar=float(K1), in1=picked[:, 1, :],
                                               op0=ALU.mult, op1=ALU.add).then_inc(topk_step, 1)
                nc.vector.tensor_scalar(gneg[:, :], top_v[:, 0:1], -1.0, None, ALU.mult).then_inc(topk_step, 1)

            def topk_gates(n, par):
                def after(k):
                    after_topk(n, k)

                dve.wait_ge(gexp_done, n + 1)
                nc.vector.reciprocal(gsum[:, :], gsum[:, :]).then_inc(topk_step, 1)
                after(28)
                nc.vector.tensor_scalar(gate[:, par, :], gexp[:, :], gsum[:, 0:1], None, ALU.mult).then_inc(topk_step, 1)
                after(29)

            def dots(n, par, g0):
                for c in range(g0, g0 + COLS):
                    dve.wait_ge(u_in[c % U_RING], 16 * (TOPK // U_RING) * n + 16 * (c // U_RING + 1))
                    nc.vector.tensor_tensor_reduce(out=u_ring[:, c % U_RING, :], in0=u_ring[:, c % U_RING, :], in1=hn[:, :],
                                                   scale=1.0, scalar=0.0, op0=ALU.mult, op1=ALU.add,
                                                   accum_out=hid[:, par, c:c + 1]).then_inc(dot_done, 1)

            def coefs(n, par, g0):
                dve.wait_ge(gelu_done, GRP * n + g0 // COLS + 1)
                nc.vector.tensor_tensor(out=coef[:, par, g0:g0 + COLS], in0=gel[:, par, g0:g0 + COLS],
                                        in1=gate[:, par, g0:g0 + COLS], op=ALU.mult).then_inc(coef_done, 1)

            def add_rows(n, par, g0):
                for c in range(g0, g0 + V_ON_VECTOR[tile_of(n)]):
                    dve.wait_ge(v_in[c % V_RING], 16 * (TOPK // V_RING) * n + 16 * (c // V_RING + 1))
                    dve.wait_ge(coef_done, GRP * n + g0 // COLS + 1)
                    if on_vector(n, c) > 1:
                        dve.wait_ge(v_added, on_vector(n, c) - 1)
                    ht = h[:, n // PH, :]
                    nc.vector.scalar_tensor_tensor(out=ht, in0=v_ring[:, c % V_RING, :], scalar=coef[:, par, c:c + 1], in1=ht,
                                                   op0=ALU.mult, op1=ALU.add).then_inc(v_added, 1)

            def hn_tile(t):
                ht = h[:, t, :] if isinstance(t, int) else h[:, bass.ds(t, 1), :].rearrange("p a n -> p (a n)")
                rt = rstd2[:, t:t + 1] if isinstance(t, int) else rstd2[:, bass.ds(t, 1)]
                nc.vector.scalar_tensor_tensor(out=hn[:, :], in0=ht, scalar=rt, in1=g2b[:, :], op0=ALU.mult, op1=ALU.mult).then_inc(hn_ready, 1)
                dve.wait_ge(hn_ready, t + 1)

            def fin_tile(t):
                last = (PH * t + PH - 1, TOPK - 1)
                if isinstance(t, int):
                    dve.wait_ge(v_used, on_tensor(PH * t + PH - 1, TOPK - 1))
                else:
                    dve.wait_ge(v_used, on_tensor(PH * t + PH, -1))
                dve.nop(nofuse=True)
                if isinstance(t, int) and on_vector(*last):
                    dve.wait_ge(v_added, on_vector(*last))
                elif not isinstance(t, int):
                    dve.wait_ge(v_added, on_vector(PH * len(HOST_TILES), -1))
                if not (isinstance(t, int) and t == 0):
                    dve.wait_ge(out_done, 16 * t)
                    dve.nop(nofuse=True)
                for half in range(2):
                    cols = slice(half * BANK, (half + 1) * BANK)
                    ht = h[:, t, cols] if isinstance(t, int) else h[:, bass.ds(t, 1), cols].rearrange("p a n -> p (a n)")
                    nc.vector.tensor_tensor(out=fin[:, cols], in0=acc[half][:, :], in1=ht, op=ALU.add).then_inc(acc_drained, 1)
                dve.wait_ge(acc_drained, 2 * t + 2)
                nc.vector.tensor_tensor_reduce(out=xs[:, :], in0=fin[:, :], in1=fin[:, :], scale=1.0, scalar=0.0,
                                               op0=ALU.mult, op1=ALU.add, accum_out=stat[:, 6:7]).then_inc(fin_step, 1)
                dve.wait_ge(fin_root, t + 1)
                nc.vector.reciprocal(fin_inv[:, :], stat[:, 7:8]).then_inc(fin_step, 1)
                dve.wait_ge(fin_step, FIN * t + 2)
                nc.vector.scalar_tensor_tensor(out=fin[:, :], in0=fin[:, :], scalar=fin_inv[:, 0:1], in1=gfb[:, :],
                                               op0=ALU.mult, op1=ALU.mult).then_inc(fin_step, 1)

            nc.vector.memset(ones[:, :], 1.0)
            nc.vector.memset(ones_row[:, :], 1.0)
            nc.vector.memset(eps[:, :], EPS)
            nc.vector.memset(selq[:, :, :], 0.0)
            link(nc.vector.memset(caug[:, :], 0.0))
            dve.wait_ge(pool_const, 6)
            for lo in (0, HD):
                nc.vector.memset(caug[lo + 32:lo + 40, :], 1.0)
                nc.vector.tensor_copy(selq[lo:lo + FH, :, :], ident[0:FH, 0:FH].unsqueeze(2).broadcast_to([FH, FH, P]))
            nc.vector.tensor_copy(iota_f[:, :], iota_i[:, :])
            link(nc.vector.tensor_copy(dist[:, :], fin[:, 0:SEQ].bitcast(I32)))
            link(nc.vector.scalar_tensor_tensor(out=dist[:, :], in0=dist[:, :], scalar=-1.0, in1=dist[:, :], op0=ALU.mult, op1=ALU.max))
            link(nc.vector.tensor_scalar(dist[0:CHUNK, SEQ - CHUNK:SEQ], dist[0:CHUNK, SEQ - CHUNK:SEQ], BIG, None, ALU.add))
            bk = mm_wait(("gain1",))
            nc.vector.tensor_copy(g1c[:, :], bk[:, 0:KC]).then_inc(mm_drained, 1)
            dve.wait_ge(mm_drained, mm_done(("gain1",)))

            for p_ in PIECES[0]:
                piece(*p_)
            dve.wait_ge(mm_drained, mm_done(("keys", PH - 1, 0)))

            def topk_all(n, par):
                topk_first(n, par)
                topk_second(n, par)
                topk_gates(n, par)

            topk_all(0, 0)
            for tile in sorted(HOST_TILES.values()):
                hn_tile(tile)
                for head in range(PH):
                    for grp in range(GRP):
                        n = PH * tile + head
                        dots(n, head % 2, grp * COLS)
                        coefs(n, head % 2, grp * COLS)
                        if tile and head == 0 and grp == 0:
                            fin_tile(tile - 1)
                        add_rows(n, head % 2, grp * COLS)
                        nxt = (n + 1, (head + 1) % 2)
                        if head < PH - 1:
                            if grp == 0:
                                topk_first(*nxt)
                            elif grp == 1:
                                topk_second(*nxt)
                            elif grp == 2:
                                topk_gates(*nxt)
                        for p_ in pieces_after(tile, head, grp):
                            piece(*p_)
                        if head == PH - 1 and grp == GRP - 1:
                            dve.wait_ge(mm_drained, mm_done(("keys", PH - 1, GROUPS[tile + 1][-1])))
                            topk_all(*nxt)
            rest = len(HOST_TILES)
            with dve.Fori(rest, TILES) as t:
                hn_tile(t)
                for par in range(2):
                    for grp in range(GRP):
                        n = PH * t + par
                        dots(n, par, grp * COLS)
                        coefs(n, par, grp * COLS)
                        if par == 0 and grp == 0:
                            fin_tile(t - 1)
                        if grp == 0:
                            topk_first(n + 1, 1 - par)
                        elif grp == 1:
                            topk_second(n + 1, 1 - par)
                        elif grp == 2:
                            topk_gates(n + 1, 1 - par)
                with dve.Fori(1, PH // 2) as i:
                    for par in range(2):
                        for grp in range(GRP):
                            n = PH * t + 2 * i + par
                            dots(n, par, grp * COLS)
                            coefs(n, par, grp * COLS)
                            if grp == 0:
                                topk_first(n + 1, 1 - par)
                            elif grp == 1:
                                topk_second(n + 1, 1 - par)
                            elif grp == 2:
                                topk_gates(n + 1, 1 - par)
            fin_tile(TILES - 1)


_INS = ['x', 'norm1_g', 'w_in', 'b_f', 'lambda_q1', 'lambda_k1', 'lambda_q2', 'lambda_k2', 'subln_g', 'w_out',
        'norm2_g', 'peer_w_q', 'peer_sub_keys', 'peer_u', 'peer_v', 'final_g']


def kernel(**inputs):
    import numpy as _np
    import concourse.bacc as _bacc
    from concourse import mybir as _mybir
    from concourse.bass_utils import run_bass_kernel_spmd as _run

    nc = _bacc.Bacc("TRN2", target_bir_lowering=False, num_devices=1)
    arrays, args = {}, []
    for name in _INS:
        a = _np.ascontiguousarray(inputs[name])
        arrays[f"in_{name}_dram"] = a
        args.append(nc.dram_tensor(f"in_{name}_dram", a.shape, _mybir.dt.from_np(a.dtype), kind="ExternalInput").ap())
    shape = inputs['x'].shape
    args.append(nc.dram_tensor("out_0_dram", shape, _mybir.dt.from_np(_np.dtype('float32')), kind="ExternalOutput").ap())
    build(nc, *args)
    r = _run(nc, [arrays], core_ids=[0])
    return r.results[0]["out_0_dram"]
```

```python
import math
from contextlib import ExitStack

import concourse.bass as bass
from concourse import mybir

F32 = mybir.dt.float32
I32 = mybir.dt.int32
U32 = mybir.dt.uint32
ALU = mybir.AluOpType
ACT = mybir.ActivationFunctionType
AX = mybir.AxisListType.X

P = 128
HALF_BANK = 256
BANK = 512
EPS = 1e-6
BIG = 1e30
HUGE = 3e38
LAMBDA_INIT = 0.8 - 0.6 * math.exp(-0.3 * 0)

GROUPS = [[0], [1, 2, 3]]
HOSTS = 1
SHARE_ATTEND = [1.5, 2.5, 4.5, 6.0]
SHARE_ROWS = 4.6
SHARE_COLS = (1.0, 2.2)
EARLY_HEADS = 2
COLS = 4
U_RING = 4
V_RING = 4
W_RING = 2
S_RING = 6


def build(nc, x, norm1_g, w_in, b_f, lambda_q1, lambda_k1, lambda_q2, lambda_k2, subln_g, w_out,
          norm2_g, peer_w_q, peer_sub_keys, peer_u, peer_v, final_g, out):
    _, SEQ, D = x.shape
    KC = D // P
    FH = b_f.shape[1]
    HD = lambda_q1.shape[1]
    DH = subln_g.shape[1]
    NDH = D // 2 // DH
    FW = FH * HD
    TILES = SEQ // P
    PH, K1 = peer_sub_keys.shape[1], peer_sub_keys.shape[3]
    TOPK = 16
    SLAB = HALF_BANK
    CHUNK = 64
    slopes = [2.0 ** (-8.0 * (i + 1) / NDH) for i in range(NDH)]
    HEADS = TILES * PH
    max_n = P * max(len(g) for g in GROUPS)

    in_kinds = []
    for kind, base in (("qa", 0), ("ka", FW), ("va", 2 * FW),
                       ("qb", 3 * FW + FH), ("kb", 4 * FW + FH), ("vb", 5 * FW + FH)):
        for c in range(0, FW, SLAB):
            in_kinds.append((kind, base + c, c))
    slab_src = ([w_in[0][:, c:c + SLAB] for _, c, _ in in_kinds]
                + [w_out[0][:, c:c + SLAB] for c in range(0, D, SLAB)]
                + [peer_w_q[0][:, c:c + SLAB] for c in range(0, PH * 2 * P, SLAB)])
    N_IN, N_OUT = len(in_kinds), D // SLAB
    SLABS = len(slab_src)

    ITEMS = FH + NDH
    MAPS = FH + 2 * NDH

    def maps_of(item):
        return [item] if item < FH else [FH + 2 * (item - FH), FH + 2 * (item - FH) + 1]

    def item_of(m):
        return m if m < FH else FH + (m - FH) // 2

    STEPS = ITEMS + 3

    def parts_of(g, s):
        return list(range(len(GROUPS[g]))) if in_kinds[s][0] in ("va", "vb") else [0, 1]

    def pieces_of(g):
        ps = []
        for t in GROUPS[g]:
            ps += [("norm1", g, t), ("xT", g, t)]
        ps += [("project", g, s, q) for s in range(4) for q in parts_of(g, s)] + [("forget", g)]
        if g == 0:
            ps += [("lambda",)]
        ps += [("project", g, s, q) for s in range(4, N_IN) for q in parts_of(g, s)]
        for t in GROUPS[g]:
            ps += [("attend", t, s) for s in range(STEPS)] + [("mix", g, t), ("mixT", g, t)]
        ps += [("outproj", g, s, t) for s in range(N_OUT) for t in GROUPS[g]]
        for t in GROUPS[g]:
            ps += [("norm2", g, t), ("hT", g, t)]
        if g == 0:
            ps += [("subkeys",)]
        for hd in range(PH):
            ps += [("query", g, 2 * hd)]
            if hd > 0:
                ps += [("keys", g, hd - 1)]
            ps += [("query", g, 2 * hd + 1)]
        return ps + [("keys", g, PH - 1)]

    GRP = TOPK // COLS
    SLOTS = HOSTS * PH * GRP - 1
    GAPS = 2 * COLS + 1
    first_pieces = pieces_of(0)
    cut_at = first_pieces.index(("keys", 0, EARLY_HEADS - 1)) + 1
    BEFORE, later = first_pieces[:cut_at], first_pieces[cut_at:] + pieces_of(1)

    def share(p):
        kind, tiles = p[0], len(GROUPS[p[1]]) if len(p) > 1 and p[0] != "attend" else 1
        if kind == "attend":
            return SHARE_ATTEND[p[1]]
        if kind in ("project", "outproj", "query"):
            by_rows = kind == "outproj" or (kind == "project" and in_kinds[p[2]][0] in ("va", "vb"))
            return SHARE_ROWS if by_rows else SHARE_COLS[0] + SHARE_COLS[1] * tiles
        return {"norm1": 4, "xT": 2, "forget": 6, "mix": 4, "mixT": 2, "norm2": 4, "hT": 2, "subkeys": 3,
                "lambda": 1, "keys": 1.0 * tiles}[kind]

    AFTER = [[] for _ in range((SLOTS + 1) * GAPS)]
    total, at = sum(share(p) for p in later), 0.0
    for p in later:
        k = min(SLOTS * GAPS - 1, int(at / total * SLOTS * GAPS))
        assert not (p[0] == "keys" and p[1] == 0) or k < (p[2] - 1) * GRP * GAPS
        AFTER[k].append(p)
        at += share(p)
    ORDER = BEFORE + [p for ps in AFTER for p in ps]

    MM = [("gain1",)]
    slab_order, slab_last_use = [], {}
    for p in ORDER:
        kind, slab_used = p[0], None
        if kind in ("xT", "mixT", "hT"):
            MM += [(kind, p[2], hf) for hf in range(2)]
        elif kind in ("forget", "lambda", "query"):
            MM.append(p)
        elif kind == "subkeys":
            MM += [("subkeys", i) for i in range(2 * PH // 4)]
        elif kind == "project":
            MM.append(p)
            slab_used = (p[1], p[2])
        elif kind == "outproj":
            MM.append(p)
            slab_used = (p[1], N_IN + p[2])
        elif kind == "keys":
            MM += [("keys", p[2], t) for t in GROUPS[p[1]]]
        if kind == "query":
            slab_used = (p[1], N_IN + N_OUT + p[2] // 2)
        if slab_used is not None:
            if slab_used not in slab_last_use:
                slab_order.append(slab_used)
            slab_last_use[slab_used] = len(MM) - 1
    mm_no = {name: i for i, name in enumerate(MM)}

    xs_no, xs_prev, reader = {}, {}, None
    for p in ORDER:
        if p[0] in ("norm1", "mix", "norm2"):
            kind, t = p[0], p[2]
            xs_no[(kind, t)] = len(xs_no) + 1
            xs_prev[(kind, t)] = reader
            if kind != "mix":
                reader = ("xT" if kind == "norm1" else "hT", t, 1)

    def mm_done(name):
        return mm_no[name] + 1

    ON_SCALAR = ("project", "mixT", "hT", "subkeys", "query", "keys")

    with ExitStack() as ctx:
        def sb(name, shape, dt=F32):
            return ctx.enter_context(nc.sbuf_tensor(name, shape, dt))

        def sem(name):
            return ctx.enter_context(nc.semaphore(name))

        h = sb("h", [P, TILES, D])
        actT = sb("actT", [P, KC, max_n])
        store = sb("store", [P, PH * 2 * K1 + KC * max_n + KC * SEQ])
        key_sc = store[:, 0:HEADS * 2 * K1].rearrange("p (h k) -> p h k", k=2 * K1)
        q_at = PH * 2 * K1
        k_at = q_at + KC * max_n
        assert k_at + KC * SEQ >= HEADS * 2 * K1
        qT = store[:, q_at:k_at].rearrange("p (c n) -> p c n", c=KC)
        kv_t = store[:, k_at:k_at + KC * SEQ].rearrange("p (c n) -> p c n", c=KC)
        v_all = sb("v_all", [P, TILES, D])
        qyT = sb("qyT", [P, 3, max_n])
        w_ring = sb("w_ring", [P, W_RING, KC, SLAB])
        xs = sb("xs", [P, D])
        hn = sb("hn", [P, D])
        fin = sb("fin", [P, D])
        u_ring = sb("u_ring", [P, U_RING, D])
        v_ring = sb("v_ring", [P, V_RING, D])
        sk_raw = u_ring[:, :, :].rearrange("p a b -> p (a b)")[:, 0:2 * PH * P].rearrange("p (c n) -> p c n", c=2 * PH)
        s_maps = sb("s_maps", [P, S_RING, SEQ])
        pT = sb("pT", [P, 2, SEQ])
        mix = sb("mix", [P, D])
        causal = sb("causal", [P, SEQ])
        dist = sb("dist", [P, SEQ])
        g2b = sb("g2b", [P, D])
        gfb = sb("gfb", [P, D])
        g1r = sb("g1r", [KC, P])
        g1c = sb("g1c", [P, KC])
        sub_c = sb("sub_c", [P, 1])
        subkT = sb("subkT", [P, 2 * PH, K1])
        ident = sb("ident", [P, P])
        diag = sb("diag", [P, COLS, P])
        wf = sb("wf", [P, KC, FH])
        bf = sb("bf", [FH, 1])
        c_all = sb("c_all", [FH, SEQ])
        z_f = sb("z_f", [FH, max_n])
        e_f = sb("e_f", [FH, max_n])
        selq = sb("selq", [P, FH, P])
        caug = sb("caug", [P, SEQ])
        ones = sb("ones", [P, 1])
        eps = sb("eps", [P, 1])
        ones_row = sb("ones_row", [1, P])
        lam_in = sb("lam_in", [1, 4, HD])
        lam_s = sb("lam_s", [1, 8])
        neglam = sb("neglam", [P, 1])
        stat = sb("stat", [P, 16])
        rstd2 = sb("rstd2", [P, TILES])
        negmax = sb("negmax", [P, MAPS])
        rowsum = sb("rowsum", [P, MAPS])
        rinv = sb("rinv", [P, MAPS])
        iota_i = sb("iota_i", [P, 16], I32)
        iota_f = sb("iota_f", [P, 16])
        tk_v = sb("tk_v", [P, 2, TOPK])
        tk_i = sb("tk_i", [P, 2, TOPK], U32)
        tk_if = sb("tk_if", [P, 2, TOPK])
        tk_s = sb("tk_s", [P, 2, K1])
        tk_w = sb("tk_w", [P, 2, K1])
        cand = sb("cand", [P, TOPK, TOPK])
        top_v = sb("top_v", [P, TOPK])
        top_p = sb("top_p", [P, TOPK], U32)
        top_hl = sb("top_hl", [P, 2, TOPK], U32)
        top_hlf = sb("top_hlf", [P, 2, TOPK])
        onehot = sb("onehot", [P, 2 * TOPK, TOPK])
        cand_w = onehot[:, 0:TOPK, :]
        picked = sb("picked", [P, 2, TOPK])
        eidx = [sb(f"eidx{i}", [P, TOPK], I32) for i in range(2)]
        gneg = sb("gneg", [P, 1])
        gexp = sb("gexp", [P, TOPK])
        fin_inv = sb("fin_inv", [P, 1])
        gsum = sb("gsum", [P, 1])
        gate = sb("gate", [P, 2, TOPK])
        hid = sb("hid", [P, 2, TOPK])
        gel = sb("gel", [P, 2, TOPK])
        coef = sb("coef", [P, 2, TOPK])

        def bank(name):
            return ctx.enter_context(nc.psum_tensor(name, [P, BANK], F32))

        acc = [bank("acc0"), bank("acc1")]
        mm = [bank("mm0"), bank("mm1")] + acc
        sc_b = [bank("sc0"), bank("sc1")]
        tr_b = bank("tr")
        o_b = bank("o")

        x_in = [sem(f"x_in{t}") for t in range(TILES)]
        consts_in = sem("consts_in")
        g1_in = sem("g1_in")
        gains_in = sem("gains_in")
        slab_in = [sem(f"slab_in{i}") for i in range(W_RING)]
        pool_const = sem("pool_const")
        dve_const = sem("dve_const")
        mm_full = sem("mm_full")
        mm_copied = sem("mm_copied")
        mm_drained = sem("mm_drained")
        xs_ready = sem("xs_ready")
        act_norm = sem("act_norm")
        dve_chain = sem("dve_chain")
        norm_ask = sem("norm_ask")
        selq_ready = sem("selq_ready")
        sc_full, sc_drained = sem("sc_full"), sem("sc_drained")
        exp_done = sem("exp_done")
        comb_done = sem("comb_done")
        tr_full, tr_drained = sem("tr_full"), sem("tr_drained")
        pv_done = sem("pv_done")
        o_drained = sem("o_drained")
        topk_step = sem("topk_step")
        gexp_done = sem("gexp_done")
        u_in = [sem(f"u_in{i}") for i in range(U_RING)]
        v_in = [sem(f"v_in{i}") for i in range(V_RING)]
        dot_done = sem("dot_done")
        gelu_done = sem("gelu_done")
        coef_done = sem("coef_done")
        diag_done = sem("diag_done")
        v_used = sem("v_used")
        acc_drained = sem("acc_drained")
        fin_step = sem("fin_step")
        fin_root = sem("fin_root")
        hn_ready = sem("hn_ready")
        out_done = sem("out_done")

        def emptied(name):
            scalar = name[0] in ON_SCALAR
            count = sum((u[0] in ON_SCALAR) == scalar for u in MM[:mm_no[name] + 1])
            return (mm_copied if scalar else mm_drained), count

        def pieces_in(n, grp, gap):
            return AFTER[(n * GRP + grp) * GAPS + gap]

        TK = 29
        TK_IDX = 26
        TK_NEG = 27
        FIN = 3

        block = ctx.enter_context(nc.Block())

        @block.sync
        def _(sp):
            sp.dma_start(h[:, 0, :], x[0, 0:P, :]).then_inc(x_in[0], 16)
            sp.dma_start(g1r[:, :], norm1_g[0].rearrange("(c p) -> c p", p=P)).then_inc(g1_in, 16)
            def load_slab(n):
                g, sl = slab_order[n]
                if n >= W_RING:
                    sp.wait_ge(mm_full, slab_last_use[slab_order[n - W_RING]] + 1)
                sp.dma_start(w_ring[:, n % W_RING, :, :],
                             slab_src[sl].rearrange("(c p) n -> p c n", p=P)).then_inc(slab_in[n % W_RING], 16)

            for n in range(W_RING):
                load_slab(n)
            sp.dma_start(sk_raw, peer_sub_keys[0].rearrange("h s k d -> k (h s) d")).then_inc(consts_in, 16)
            for i, v in enumerate((lambda_q1, lambda_q2, lambda_k1, lambda_k2)):
                sp.dma_start(lam_in[:, i, :], v).then_inc(consts_in, 16)
            sp.dma_start(sub_c[:, :], subln_g.rearrange("a p -> p a")).then_inc(consts_in, 16)
            sp.dma_start(wf[:, :, :], w_in[0][:, 3 * FW:3 * FW + FH].rearrange("(c p) n -> p c n", p=P)).then_inc(consts_in, 16)
            sp.dma_start(bf[:, :], b_f.rearrange("a p -> p a")).then_inc(consts_in, 16)

            sp.dma_start(g2b[:, :], norm2_g.broadcast_to([P, D])).then_inc(gains_in, 16)
            sp.dma_start(gfb[:, :], final_g.rearrange("(a n) -> a n", a=1).broadcast_to([P, D])).then_inc(out_done, 16)
            for t in range(1, TILES):
                sp.dma_start(h[:, t, :], x[0, t * P:(t + 1) * P, :]).then_inc(x_in[t], 16)
            for n in range(W_RING, len(slab_order)):
                load_slab(n)

            with sp.Fori(0, TILES) as t:
                sp.wait_ge(fin_step, FIN * t + FIN)
                sp.dma_start(out[0, bass.ds(t * P, P), :], fin[:, :]).then_inc(out_done, 16)
            sp.wait_ge(out_done, 16 * (TILES + 1))

        @block.gpsimd
        def _(pool):
            nc.gpsimd.memset(ident[:, :], 0.0).then_inc(pool_const, 1)
            nc.gpsimd.memset(causal[:, :], 0.0).then_inc(pool_const, 1)
            nc.gpsimd.iota(fin[:, 0:SEQ].bitcast(I32), pattern=[[1, SEQ]], base=-(SEQ - P), channel_multiplier=-1).then_inc(pool_const, 1)
            nc.gpsimd.iota(iota_i[:, :], pattern=[[1, TOPK]], base=0, channel_multiplier=0).then_inc(pool_const, 1)
            pool.wait_ge(pool_const, 4)
            nc.gpsimd.affine_select(out=ident[:, :], in_=ident[:, :], compare_op=ALU.not_equal, fill=1.0,
                                    base=0, pattern=[[-1, P]], channel_multiplier=1).then_inc(pool_const, 1)
            nc.gpsimd.affine_select(out=causal[:, SEQ - P:SEQ], in_=causal[:, SEQ - P:SEQ], compare_op=ALU.is_ge, fill=-BIG,
                                    base=0, pattern=[[-1, P]], channel_multiplier=1).then_inc(pool_const, 1)

            def gathers(n, par, first):
                pool.wait_ge(topk_step, TK * n + TK_IDX)
                pool.nop(nofuse=True)
                for g0 in range(0, TOPK, COLS):
                    for c in range(g0, g0 + COLS):
                        if not (first and c < U_RING):
                            pool.wait_ge(dot_done, TOPK * n + c + 1 - U_RING)
                            pool.nop(nofuse=True)
                        nc.gpsimd.indirect_dma_start(
                            out=u_ring[:, c % U_RING, :], out_offset=None, in_=peer_u[0],
                            in_offset=bass.IndirectOffsetOnAxis(ap=eidx[par][:, c:c + 1], axis=0)).then_inc(u_in[c % U_RING], 16)
                    for c in range(g0, g0 + COLS):
                        if not (first and c < V_RING):
                            pool.wait_ge(v_used, TOPK * n + c + 1 - V_RING)
                            pool.nop(nofuse=True)
                        nc.gpsimd.indirect_dma_start(
                            out=v_ring[:, c % V_RING, :], out_offset=None, in_=peer_v[0],
                            in_offset=bass.IndirectOffsetOnAxis(ap=eidx[par][:, c:c + 1], axis=0)).then_inc(v_in[c % V_RING], 16)

            for n in range(PH * HOSTS):
                gathers(n, n % 2, n == 0)
            with pool.Fori(PH * HOSTS // 2, HEADS // 2) as i:
                for par in range(2):
                    gathers(2 * i + par, par, False)

        @block.tensor
        def _(pe):
            def mm_bank(name):
                n = mm_no[name]
                if n >= len(mm):
                    pe.wait_ge(*emptied(MM[n - len(mm)]))
                return mm[n % len(mm)]

            def transposes(name, src):
                b = mm_bank(name)
                for j in range(4):
                    last = nc.tensor.transpose(b[:, j * P:(j + 1) * P], src(j), ident[:, :])
                last.then_inc(mm_full, 1)

            def slab(g, sl):
                n = slab_order.index((g, sl))
                pe.wait_ge(slab_in[n % W_RING], 16 * (n // W_RING + 1))
                return w_ring[:, n % W_RING, :, :]

            def rows_out(name, j, w):
                bk = mm_bank(name)
                for c in range(KC):
                    last = nc.tensor.matmul(bk[:, 0:SLAB], actT[:, c, j * P:(j + 1) * P], w[:, c, :],
                                            start=(c == 0), stop=(c == KC - 1))
                last.then_inc(mm_full, 1)

            def cols_out(name, n, w, q):
                bk = mm_bank(name)
                for c in range(KC):
                    last = nc.tensor.matmul(bk[:, 0:n], w[:, c, q * P:(q + 1) * P], actT[:, c, 0:n],
                                            start=(c == 0), stop=(c == KC - 1))
                last.then_inc(mm_full, 1)

            def piece(kind, *p):
                if kind == "xT":
                    pe.wait_ge(xs_ready, xs_no[("norm1", p[1])])
                    for hf in range(2):
                        transposes(("xT", p[1], hf), lambda j: xs[:, (4 * hf + j) * P:(4 * hf + j + 1) * P])
                elif kind == "project":
                    g, sl, q = p
                    w = slab(g, sl)
                    pe.wait_ge(*emptied(("xT", GROUPS[g][-1], 1)))
                    if in_kinds[sl][0] in ("va", "vb"):
                        rows_out((kind, *p), q, w)
                    else:
                        cols_out((kind, *p), P * len(GROUPS[g]), w, q)
                elif kind == "forget":
                    n = P * len(GROUPS[p[0]])
                    pe.wait_ge(consts_in, 16 * 8)
                    bk = mm_bank((kind, *p))
                    for c in range(KC):
                        last = nc.tensor.matmul(bk[0:FH, 0:n], wf[:, c, :], actT[:, c, 0:n], start=(c == 0), stop=(c == KC - 1))
                    last.then_inc(mm_full, 1)
                elif kind == "lambda":
                    pe.wait_ge(dve_const, 1)
                    nc.tensor.matmul(mm_bank(("lambda",))[:, 0:1], ones_row[:, :], lam_s[0:1, 4:5],
                                     start=True, stop=True).then_inc(mm_full, 1)
                elif kind == "subkeys":
                    for i in range(2 * PH // 4):
                        transposes(("subkeys", i), lambda j: sk_raw[:, 4 * i + j, :])
                elif kind == "attend":
                    attend(*p)
                elif kind == "mixT":
                    t = p[1]
                    for hf in range(2):
                        if hf == 0:
                            pe.wait_ge(o_drained, 2 * t + 1)
                        else:
                            pe.wait_ge(xs_ready, xs_no[("mix", t)])
                        transposes(("mixT", t, hf), lambda j: mix[:, (4 * hf + j) * P:(4 * hf + j + 1) * P])
                elif kind == "outproj":
                    g, sl, t = p
                    w = slab(g, N_IN + sl)
                    pe.wait_ge(*emptied(("mixT", t, 1)))
                    rows_out((kind, *p), GROUPS[g].index(t), w)
                elif kind == "hT":
                    pe.wait_ge(xs_ready, xs_no[("norm2", p[1])])
                    for hf in range(2):
                        transposes(("hT", p[1], hf), lambda j: xs[:, (4 * hf + j) * P:(4 * hf + j + 1) * P])
                elif kind == "query":
                    g, c2 = p
                    pe.wait_ge(*emptied(("hT", GROUPS[g][-1], 1)))
                    cols_out((kind, *p), P * len(GROUPS[g]), slab(g, N_IN + N_OUT + c2 // 2), c2 % 2)
                elif kind == "keys":
                    g, hd = p
                    pe.wait_ge(*emptied(("query", g, 2 * hd + 1)))
                    for j, t in enumerate(GROUPS[g]):
                        bk = mm_bank(("keys", hd, t))
                        for sd in range(2):
                            c2 = 2 * hd + sd
                            last = nc.tensor.matmul(bk[:, sd * K1:(sd + 1) * K1], qyT[:, c2 % 3, j * P:(j + 1) * P], subkT[:, c2, :],
                                                    start=True, stop=True)
                        last.then_inc(mm_full, 1)

            def attend(t, step):
                nk = P * (t + 1)
                g = next(i for i, ts in enumerate(GROUPS) if t in ts)
                j = GROUPS[g].index(t)
                if step == 0:
                    pe.wait_ge(*emptied(("project", g, N_IN - 1, len(GROUPS[g]) - 1)))
                    pe.wait_ge(selq_ready, 2 * (t + 1))
                if step < ITEMS:
                    for m in maps_of(step):
                        k = MAPS * t + m
                        if k >= 2:
                            pe.wait_ge(sc_drained, k - 1)
                        bk = sc_b[k % 2]
                        if m < FH:
                            lo, ch = HD * (m % 2), m // 2
                        else:
                            lo, ch = HD * ((m - FH) % 2), KC // 2 + (m - FH) // 2
                        mo = nc.tensor.matmul(bk[:, 0:nk], qT[lo:lo + HD, ch, j * P:(j + 1) * P], kv_t[lo:lo + HD, ch, 0:nk],
                                              start=True, stop=(m >= FH))
                        if m < FH:
                            mo = nc.tensor.matmul(bk[:, 0:nk], selq[lo:lo + 40, m, :], caug[lo:lo + 40, 0:nk], start=False, stop=True)
                        mo.then_inc(sc_full, 1)
                it = step - 2
                if 0 <= it < ITEMS:
                    k = ITEMS * t + it
                    if it < FH:
                        pe.wait_ge(exp_done, MAPS * t + it + 1)
                    else:
                        pe.wait_ge(comb_done, NDH * t + it - FH + 1)
                    if k >= 1:
                        pe.wait_ge(tr_drained, k)
                    slot = (MAPS * t + maps_of(it)[0]) % S_RING
                    for q in range(t + 1):
                        last = nc.tensor.transpose(tr_b[:, q * P:(q + 1) * P], s_maps[:, slot, q * P:(q + 1) * P], ident[:, :])
                    last.then_inc(tr_full, 1)
                it = step - 3
                if 0 <= it < ITEMS:
                    k = ITEMS * t + it
                    pe.wait_ge(tr_drained, k + 1)
                    if it == 0 and t > 0:
                        pe.wait_ge(o_drained, 2 * t)
                    if it == FH:
                        pe.wait_ge(o_drained, 2 * t + 1)
                    w = HD if it < FH else DH
                    col = HD * it if it < FH else DH * (it - FH)
                    vcol = col if it < FH else FW + col
                    for q in range(t + 1):
                        last = nc.tensor.matmul(o_b[:, col:col + w], pT[:, k % 2, q * P:(q + 1) * P], v_all[:, q, vcol:vcol + w],
                                                start=(q == 0), stop=(q == t))
                    last.then_inc(pv_done, 1)

            def peer_group(n, g0, starts, emptied):
                for c in range(g0, g0 + COLS):
                    if c == 0 and emptied is not None:
                        pe.wait_ge(acc_drained, emptied)
                    pe.wait_ge(v_in[c % V_RING], 16 * (TOPK // V_RING) * n + 16 * (c // V_RING + 1))
                    pe.wait_ge(diag_done, TOPK * (n - PH * HOSTS) + c + 1)
                    for half in range(2):
                        last = nc.tensor.matmul(acc[half][:, :], diag[:, c % COLS, :], v_ring[:, c % V_RING, half * BANK:(half + 1) * BANK],
                                                start=(starts and c == 0), stop=False, skip_group_check=True)
                    last.then_inc(v_used, 1)

            pe.wait_ge(pool_const, 6)
            pe.wait_ge(g1_in, 16)
            nc.tensor.transpose(mm_bank(("gain1",))[:, 0:KC], g1r[:, :], ident[0:KC, 0:KC]).then_inc(mm_full, 1)
            for p_ in BEFORE:
                piece(*p_)
            for tile in range(HOSTS):
                for n in range(PH * tile, PH * tile + PH):
                    for grp in range(GRP):
                        for gap in range(GAPS):
                            for p_ in pieces_in(n, grp, gap):
                                piece(*p_)
            with pe.Fori(HOSTS, TILES) as t:
                for par in range(2):
                    for grp in range(GRP):
                        peer_group(PH * t + par, grp * COLS, par == 0, 2 * t if par == 0 else None)
                with pe.Fori(1, PH // 2) as i:
                    for par in range(2):
                        for grp in range(GRP):
                            peer_group(PH * t + 2 * i + par, grp * COLS, False, None)

        @block.scalar
        def _(act):
            asked = [0]
            given = [0]

            def mm_wait(name):
                act.wait_ge(mm_full, mm_done(name))
                return mm[mm_no[name] % len(mm)]

            def four(b):
                return b[:, :].rearrange("p (c n) -> p c n", c=4)

            def root(dst, src, scale, count=None):
                asked[0] += 1
                given[0] += 1
                act.wait_ge(norm_ask, asked[0])
                nc.scalar.activation(dst, src, ACT.Sqrt, scale=scale, bias=eps[:, 0:1]).then_inc(act_norm, 1)

            def piece(kind, *p):
                if kind == "norm1":
                    root(stat[:, 1:2], stat[:, 0:1], 1.0 / D)
                elif kind == "norm2":
                    root(stat[:, 5:6], stat[:, 4:5], 1.0 / D)
                elif kind == "mix":
                    root(stat[:, 12:12 + NDH], stat[:, 8:8 + NDH], 1.0 / DH)
                elif kind == "project":
                    g, sl, q = p
                    n = P * len(GROUPS[g])
                    knd, _, col = in_kinds[sl]
                    bk = mm_wait((kind, *p))
                    if knd in ("va", "vb"):
                        col += FW if knd == "vb" else 0
                        nc.scalar.activation(v_all[:, GROUPS[g][q], col:col + SLAB], bk[:, 0:SLAB], ACT.Copy).then_inc(mm_copied, 1)
                    else:
                        ch = col // P + q + (KC // 2 if knd in ("qb", "kb") else 0)
                        if knd in ("ka", "kb"):
                            t0 = GROUPS[g][0] * P
                            nc.scalar.activation(kv_t[:, ch, t0:t0 + n], bk[:, 0:n], ACT.Copy).then_inc(mm_copied, 1)
                        else:
                            f = HD ** -0.5 if knd == "qa" else -(HD ** -0.5) / slopes[ch - KC // 2]
                            nc.scalar.activation(qT[:, ch, 0:n], bk[:, 0:n], ACT.Copy, scale=f).then_inc(mm_copied, 1)
                elif kind == "subkeys":
                    for i in range(2 * PH // 4):
                        bk = mm_wait(("subkeys", i))
                        nc.scalar.activation(subkT[:, 4 * i:4 * i + 4, :], four(bk), ACT.Copy).then_inc(mm_copied, 1)
                elif kind == "mixT":
                    g, t = p
                    j = GROUPS[g].index(t)
                    bk = mm_wait(("mixT", t, 0))
                    nc.scalar.activation(actT[:, 0:4, j * P:(j + 1) * P], four(bk), ACT.Copy).then_inc(mm_copied, 1)
                    bk = mm_wait(("mixT", t, 1))
                    act.wait_ge(dve_const, 1)
                    nc.scalar.activation(actT[:, 4:8, j * P:(j + 1) * P], four(bk), ACT.Copy, scale=sub_c[:, 0:1]).then_inc(mm_copied, 1)
                elif kind == "hT":
                    g, t = p
                    j = GROUPS[g].index(t)
                    if j == 0:
                        act.wait_ge(mm_full, mm_done(("outproj", g, N_OUT - 1, GROUPS[g][-1])))
                    for hf in range(2):
                        bk = mm_wait(("hT", t, hf))
                        nc.scalar.activation(actT[:, 4 * hf:4 * hf + 4, j * P:(j + 1) * P], four(bk), ACT.Copy).then_inc(mm_copied, 1)
                elif kind == "query":
                    g, c2 = p
                    n = P * len(GROUPS[g])
                    bk = mm_wait((kind, *p))
                    nc.scalar.activation(qyT[:, c2 % 3, 0:n], bk[:, 0:n], ACT.Copy).then_inc(mm_copied, 1)
                elif kind == "keys":
                    g, hd = p
                    for t in GROUPS[g]:
                        bk = mm_wait(("keys", hd, t))
                        nc.scalar.activation(key_sc[:, PH * t + hd, :], bk[:, 0:2 * K1], ACT.Copy).then_inc(mm_copied, 1)
                elif kind == "lambda":
                    asked[0] += 1
                    given[0] += 1
                    act.wait_ge(norm_ask, asked[0])
                    nc.scalar.activation(lam_s[0:1, 2:4], lam_s[0:1, 0:2], ACT.Exp).then_inc(act_norm, 1)
                elif kind == "forget":
                    n = P * len(GROUPS[p[0]])
                    asked[0] += 1
                    act.wait_ge(norm_ask, asked[0])
                    nc.scalar.activation(e_f[:, 0:n], e_f[:, 0:n], ACT.Exp, scale=-1.0).then_inc(act_norm, 1)
                    given[0] += 2
                    act.wait_ge(act_norm, given[0] - 1)
                    nc.scalar.activation(e_f[:, 0:n], e_f[:, 0:n], ACT.Ln, bias=1.0).then_inc(act_norm, 1)
                elif kind == "attend":
                    t, step = p
                    nk = P * (t + 1)
                    if step < ITEMS:
                        for m in maps_of(step):
                            k = MAPS * t + m
                            act.wait_ge(sc_drained, k + 1)
                            s = s_maps[:, k % S_RING, 0:nk]
                            nc.scalar.activation(s, s, ACT.Exp, scale=-1.0, bias=negmax[:, m:m + 1],
                                                 accum_out=rowsum[:, m:m + 1]).then_inc(exp_done, 1)
                    it = step - 2
                    if 0 <= it < ITEMS:
                        k = ITEMS * t + it
                        act.wait_ge(tr_full, k + 1)
                        if k >= 2:
                            act.wait_ge(pv_done, k - 1)
                        nc.scalar.activation(pT[:, k % 2, 0:nk], tr_b[:, 0:nk], ACT.Copy).then_inc(tr_drained, 1)

            def gate_exp(n):
                act.wait_ge(topk_step, TK * n + TK_NEG)
                nc.scalar.activation(gexp[:, :], top_v[:, :], ACT.Exp, bias=gneg[:, 0:1], accum_out=gsum[:, 0:1]).then_inc(gexp_done, 1)

            def gelu(n, par, g0):
                act.wait_ge(dot_done, TOPK * n + g0 + COLS)
                nc.scalar.activation(gel[:, par, g0:g0 + COLS], hid[:, par, g0:g0 + COLS], ACT.Gelu).then_inc(gelu_done, 1)

            def peer_group(n, par, g0):
                gelu(n, par, g0)
                act.wait_ge(coef_done, GRP * n + g0 // COLS + 1)
                for c in range(COLS):
                    act.wait_ge(v_used, TOPK * n + g0 + c + 1 - COLS)
                    nc.scalar.activation(diag[:, c, :], ident[:, :], ACT.Copy,
                                         scale=coef[:, par, g0 + c:g0 + c + 1]).then_inc(diag_done, 1)

            def fin_rt(t):
                act.wait_ge(fin_step, FIN * t + 1)
                nc.scalar.activation(stat[:, 7:8], stat[:, 6:7], ACT.Sqrt, scale=1.0 / D, bias=eps[:, 0:1]).then_inc(fin_root, 1)

            act.wait_ge(pool_const, 6)
            for p_ in BEFORE:
                piece(*p_)
            gate_exp(0)
            for tile in range(HOSTS):
                for n in range(PH * tile, PH * tile + PH):
                    for grp in range(GRP):
                        for gap in range(GAPS):
                            if gap == COLS - 1:
                                gelu(n, n % 2, grp * COLS)
                            for p_ in pieces_in(n, grp, gap):
                                piece(*p_)
                        if tile and n == PH * tile and grp == 0:
                            fin_rt(tile - 1)
                        if grp == 2 and n < PH * tile + PH - 1:
                            gate_exp(n + 1)
                gate_exp(PH * tile + PH)
            with act.Fori(HOSTS, TILES) as t:
                for par in range(2):
                    for grp in range(GRP):
                        peer_group(PH * t + par, par, grp * COLS)
                        if par == 0 and grp == 0:
                            fin_rt(t - 1)
                        if grp == 2:
                            gate_exp(PH * t + par + 1)
                with act.Fori(1, PH // 2) as i:
                    for par in range(2):
                        for grp in range(GRP):
                            peer_group(PH * t + 2 * i + par, par, grp * COLS)
                            if grp == 2:
                                gate_exp(PH * t + 2 * i + par + 1)
            fin_rt(TILES - 1)

        @block.vector
        def _(dve):
            chain = [0]
            rooted = [0]
            handed = [0]

            def link(ins):
                chain[0] += 1
                ins.then_inc(dve_chain, 1)
                dve.wait_ge(dve_chain, chain[0])

            def from_act(ins, steps=1):
                ins.then_inc(norm_ask, 1)
                rooted[0] += steps
                dve.wait_ge(act_norm, rooted[0])

            def mm_wait(name):
                dve.wait_ge(mm_full, mm_done(name))
                return mm[mm_no[name] % len(mm)]

            def four(b):
                return b[:, :].rearrange("p (c n) -> p c n", c=4)

            def norm_rows(src, st, width_scale=None):
                from_act(nc.vector.tensor_tensor_reduce(out=xs[:, :], in0=src, in1=src, scale=1.0, scalar=0.0,
                                                        op0=ALU.mult, op1=ALU.add, accum_out=stat[:, st:st + 1]))

            def piece(kind, *p):
                if kind == "norm1":
                    g, t = p
                    dve.wait_ge(x_in[t], 16)
                    if xs_prev[("norm1", t)] is not None:
                        dve.wait_ge(mm_full, mm_done(xs_prev[("norm1", t)]))
                    norm_rows(h[:, t, :], 0)
                    link(nc.vector.reciprocal(stat[:, 2:3], stat[:, 1:2]))
                    nc.vector.tensor_scalar(xs[:, :], h[:, t, :], stat[:, 2:3], None, ALU.mult).then_inc(xs_ready, 1)
                elif kind == "xT":
                    g, t = p
                    j = GROUPS[g].index(t)
                    if j == 0 and g > 0:
                        dve.wait_ge(mm_full, mm_done(("query", g - 1, 2 * PH - 1)))
                    for hf in range(2):
                        bk = mm_wait(("xT", t, hf))
                        nc.vector.tensor_tensor(out=actT[:, 4 * hf:4 * hf + 4, j * P:(j + 1) * P], in0=four(bk),
                                                in1=g1c[:, 4 * hf:4 * hf + 4].unsqueeze(2).broadcast_to([P, 4, P]),
                                                op=ALU.mult).then_inc(mm_drained, 1)
                elif kind == "forget":
                    g, = p
                    n, t0 = P * len(GROUPS[g]), P * GROUPS[g][0]
                    dve.wait_ge(consts_in, 16 * 8)
                    bk = mm_wait(("forget", g))
                    nc.vector.tensor_scalar(z_f[:, 0:n], bk[0:FH, 0:n], bf[:, 0:1], None, ALU.add).then_inc(mm_drained, 1)
                    dve.wait_ge(*emptied(("forget", g)))
                    from_act(nc.vector.scalar_tensor_tensor(out=e_f[:, 0:n], in0=z_f[:, 0:n], scalar=-1.0, in1=z_f[:, 0:n],
                                                            op0=ALU.mult, op1=ALU.max), 2)
                    link(nc.vector.scalar_tensor_tensor(out=z_f[:, 0:n], in0=z_f[:, 0:n], scalar=0.0, in1=e_f[:, 0:n],
                                                        op0=ALU.min, op1=ALU.subtract))
                    init = 0.0 if t0 == 0 else c_all[:, t0 - 1:t0]
                    link(nc.vector.tensor_tensor_scan(c_all[:, t0:t0 + n], ones[0:FH, :].broadcast_to([FH, n]), z_f[:, 0:n],
                                                      init, ALU.mult, ALU.add))
                    for lo in (0, HD):
                        link(nc.vector.tensor_scalar(caug[lo:lo + FH, t0:t0 + n], c_all[:, t0:t0 + n], -1.0, None, ALU.mult))
                elif kind == "lambda":
                    link(nc.vector.tensor_tensor(out=lam_in[:, 0:2, :], in0=lam_in[:, 0:2, :], in1=lam_in[:, 2:4, :], op=ALU.mult))
                    from_act(nc.vector.tensor_reduce(lam_s[0:1, 0:2], lam_in[:, 0:2, :], AX, ALU.add))
                    link(nc.vector.tensor_tensor(out=lam_s[0:1, 5:6], in0=lam_s[0:1, 3:4], in1=lam_s[0:1, 2:3], op=ALU.subtract))
                    link(nc.vector.tensor_scalar(sub_c[:, :], sub_c[:, :], 1.0 - LAMBDA_INIT, None, ALU.mult))
                    nc.vector.tensor_scalar(lam_s[0:1, 4:5], lam_s[0:1, 5:6], LAMBDA_INIT, None, ALU.subtract).then_inc(dve_const, 1)
                    bk = mm_wait(("lambda",))
                    nc.vector.tensor_copy(neglam[:, :], bk[:, 0:1]).then_inc(mm_drained, 1)
                    dve.wait_ge(*emptied(("lambda",)))
                elif kind == "attend":
                    attend(*p)
                elif kind == "mix":
                    g, t = p
                    dve.wait_ge(pv_done, ITEMS * (t + 1))
                    nc.vector.tensor_copy(mix[:, FW:D], o_b[:, :]).then_inc(o_drained, 1)
                    dve.wait_ge(o_drained, 2 * t + 2)
                    if xs_prev[("mix", t)] is not None:
                        dve.wait_ge(mm_full, mm_done(xs_prev[("mix", t)]))
                    link(nc.vector.tensor_tensor(out=xs[:, 0:FW], in0=mix[:, FW:D], in1=mix[:, FW:D], op=ALU.mult))
                    from_act(nc.vector.tensor_reduce(stat[:, 8:8 + NDH], xs[:, 0:FW].rearrange("p (a n) -> p a n", a=NDH),
                                                     AX, ALU.add))
                    link(nc.vector.reciprocal(rinv[:, 0:NDH], stat[:, 12:12 + NDH]))
                    mb = mix[:, FW:D].rearrange("p (a n) -> p a n", a=NDH)
                    nc.vector.tensor_tensor(out=mb, in0=mb, in1=rinv[:, 0:NDH].unsqueeze(2).broadcast_to([P, NDH, DH]),
                                            op=ALU.mult).then_inc(xs_ready, 1)
                elif kind == "outproj":
                    g, sl, t = p
                    bk = mm_wait((kind, *p))
                    hs = h[:, t, sl * SLAB:(sl + 1) * SLAB]
                    nc.vector.tensor_tensor(out=hs, in0=bk[:, 0:SLAB], in1=hs, op=ALU.add).then_inc(mm_drained, 1)
                elif kind == "norm2":
                    g, t = p
                    dve.wait_ge(*emptied(("outproj", g, N_OUT - 1, t)))
                    dve.wait_ge(mm_full, mm_done(xs_prev[("norm2", t)]))
                    norm_rows(h[:, t, :], 4)
                    if t == 0:
                        dve.wait_ge(gains_in, 16)
                    link(nc.vector.reciprocal(rstd2[:, t:t + 1], stat[:, 5:6]))
                    nc.vector.scalar_tensor_tensor(out=xs[:, :], in0=h[:, t, :], scalar=rstd2[:, t:t + 1], in1=g2b[:, :],
                                                   op0=ALU.mult, op1=ALU.mult).then_inc(xs_ready, 1)

            def attend(t, step):
                nk = P * (t + 1)
                if step == 0:
                    if t > 0:
                        dve.wait_ge(sc_full, MAPS * t)
                    for lo in (0, HD):
                        nc.vector.tensor_tensor(out=selq[lo + 32:lo + 32 + FH, :, :],
                                                in0=c_all[:, t * P:(t + 1) * P].unsqueeze(1).broadcast_to([FH, FH, P]),
                                                in1=ident[0:FH, 0:FH].unsqueeze(2).broadcast_to([FH, FH, P]),
                                                op=ALU.mult).then_inc(selq_ready, 1)
                if step < ITEMS:
                    for m in maps_of(step):
                        k = MAPS * t + m
                        dve.wait_ge(sc_full, k + 1)
                        if k >= S_RING:
                            k0 = k - S_RING
                            dve.wait_ge(tr_full, ITEMS * (k0 // MAPS) + item_of(k0 % MAPS) + 1)
                        strip, scale = (causal, -1.0) if m < FH else (dist, slopes[(m - FH) // 2])
                        nc.vector.tensor_tensor_reduce(out=s_maps[:, k % S_RING, 0:nk], in0=sc_b[k % 2][:, 0:nk],
                                                       in1=strip[:, SEQ - nk:SEQ], scale=scale, scalar=HUGE,
                                                       op0=ALU.add, op1=ALU.min, accum_out=negmax[:, m:m + 1]).then_inc(sc_drained, 1)
                it = step - 1
                if FH <= it < ITEMS:
                    m1, m2 = maps_of(it)
                    dve.wait_ge(exp_done, MAPS * t + m2 + 1)
                    link(nc.vector.reciprocal(rinv[:, m1:m2 + 1], rowsum[:, m1:m2 + 1]))
                    link(nc.vector.tensor_scalar(rinv[:, m2:m2 + 1], rinv[:, m2:m2 + 1], neglam[:, 0:1], None, ALU.mult))
                    s1 = s_maps[:, (MAPS * t + m1) % S_RING, 0:nk]
                    s2 = s_maps[:, (MAPS * t + m2) % S_RING, 0:nk]
                    link(nc.vector.tensor_scalar(s2, s2, rinv[:, m2:m2 + 1], None, ALU.mult))
                    nc.vector.scalar_tensor_tensor(out=s1, in0=s1, scalar=rinv[:, m1:m1 + 1], in1=s2,
                                                   op0=ALU.mult, op1=ALU.add).then_inc(comb_done, 1)
                if step == FH + 2:
                    dve.wait_ge(pv_done, ITEMS * t + FH)
                    link(nc.vector.reciprocal(rinv[:, 0:FH], rowsum[:, 0:FH]))
                    if t > 0:
                        dve.wait_ge(mm_full, mm_done(("mixT", t - 1, 1)))
                    nc.vector.tensor_tensor(out=mix[:, 0:FW].rearrange("p (a n) -> p a n", a=FH),
                                            in0=o_b[:, :].rearrange("p (a n) -> p a n", a=FH),
                                            in1=rinv[:, 0:FH].unsqueeze(2).broadcast_to([P, FH, HD]),
                                            op=ALU.mult).then_inc(o_drained, 1)

            def after_topk(n, k):
                dve.wait_ge(topk_step, TK * n + k)
                dve.nop(nofuse=True)

            def topk_first(n, par):
                if isinstance(n, int):
                    dve.wait_ge(*emptied(("keys", n % PH, n // PH)))
                def after(k):
                    after_topk(n, k)

                s = key_sc[:, n, :] if isinstance(n, int) else key_sc[:, bass.ds(n % HEADS, 1), :].rearrange("p a k -> p (a k)")
                nc.vector.tensor_copy(tk_s[:, :, :].rearrange("p a k -> p (a k)"), s).then_inc(topk_step, 1)
                after(1)
                s1 = [tk_s[:, 0, :], tk_s[:, 1, :]]
                for q in range(2):
                    nc.vector.max(tk_v[:, q, 0:8], s1[q]).then_inc(topk_step, 1)
                for q in range(2):
                    after(q + 2)
                    nc.vector.match_replace(tk_w[:, q, :], tk_v[:, q, 0:8], s1[q], -HUGE).then_inc(topk_step, 1)
                for q in range(2):
                    nc.vector.max_index(tk_i[:, q, 0:8], tk_v[:, q, 0:8], s1[q]).then_inc(topk_step, 1)
                for q in range(2):
                    after(q + 4)
                    nc.vector.max(tk_v[:, q, 8:16], tk_w[:, q, :]).then_inc(topk_step, 1)
                for q in range(2):
                    after(q + 8)
                    nc.vector.max_index(tk_i[:, q, 8:16], tk_v[:, q, 8:16], tk_w[:, q, :]).then_inc(topk_step, 1)
                nc.vector.tensor_tensor(out=cand[:, :, :], in0=tk_v[:, 0, :].unsqueeze(2).broadcast_to([P, TOPK, TOPK]),
                                        in1=tk_v[:, 1, :].unsqueeze(1).broadcast_to([P, TOPK, TOPK]),
                                        op=ALU.add).then_inc(topk_step, 1)
                after(11)
                nc.vector.tensor_copy(tk_if[:, :, :], tk_i[:, :, :]).then_inc(topk_step, 1)

            def topk_second(n, par):
                def after(k):
                    after_topk(n, k)

                cf = cand[:, :, :].rearrange("p a b -> p (a b)")
                wf_ = cand_w[:, :, :].rearrange("p a b -> p (a b)")
                after(12)
                nc.vector.max(top_v[:, 0:8], cf).then_inc(topk_step, 1)
                after(14)
                nc.vector.match_replace(wf_, top_v[:, 0:8], cf, -HUGE).then_inc(topk_step, 1)
                nc.vector.max_index(top_p[:, 0:8], top_v[:, 0:8], cf).then_inc(topk_step, 1)
                after(15)
                nc.vector.max(top_v[:, 8:16], wf_).then_inc(topk_step, 1)
                after(17)
                nc.vector.max_index(top_p[:, 8:16], top_v[:, 8:16], wf_).then_inc(topk_step, 1)
                after(18)
                nc.vector.tensor_scalar(top_hl[:, 0, :], top_p[:, :], 4, None, ALU.logical_shift_right).then_inc(topk_step, 1)
                nc.vector.tensor_scalar(top_hl[:, 1, :], top_p[:, :], 15, None, ALU.bitwise_and).then_inc(topk_step, 1)
                after(20)
                nc.vector.tensor_copy(top_hlf[:, :, :], top_hl[:, :, :]).then_inc(topk_step, 1)
                after(21)
                nc.vector.tensor_tensor(out=onehot[:, :, :], in0=top_hlf[:, :, :].rearrange("p a b -> p (a b)").unsqueeze(2).broadcast_to([P, 2 * TOPK, TOPK]),
                                        in1=iota_f[:, :].unsqueeze(1).broadcast_to([P, 2 * TOPK, TOPK]),
                                        op=ALU.is_equal).then_inc(topk_step, 1)
                for q in range(2):
                    after(22)
                    oh = onehot[:, q * TOPK:(q + 1) * TOPK, :]
                    nc.vector.tensor_tensor(out=oh, in0=oh, in1=tk_if[:, q, :].unsqueeze(1).broadcast_to([P, TOPK, TOPK]),
                                            op=ALU.mult).then_inc(topk_step, 1)
                after(24)
                nc.vector.tensor_reduce(picked[:, :, :].rearrange("p a b -> p (a b)"), onehot[:, :, :], AX, ALU.add).then_inc(topk_step, 1)
                after(25)
                if not (isinstance(n, int) and n < 2):
                    dve.wait_ge(v_used, TOPK * (n - 1))
                nc.vector.scalar_tensor_tensor(out=eidx[par][:, :], in0=picked[:, 0, :], scalar=float(K1), in1=picked[:, 1, :],
                                               op0=ALU.mult, op1=ALU.add).then_inc(topk_step, 1)
                nc.vector.tensor_scalar(gneg[:, :], top_v[:, 0:1], -1.0, None, ALU.mult).then_inc(topk_step, 1)

            def topk_gates(n, par):
                def after(k):
                    after_topk(n, k)

                dve.wait_ge(gexp_done, n + 1)
                nc.vector.reciprocal(gsum[:, :], gsum[:, :]).then_inc(topk_step, 1)
                after(28)
                nc.vector.tensor_scalar(gate[:, par, :], gexp[:, :], gsum[:, 0:1], None, ALU.mult).then_inc(topk_step, 1)
                after(29)

            def dot(n, par, c):
                dve.wait_ge(u_in[c % U_RING], 16 * (TOPK // U_RING) * n + 16 * (c // U_RING + 1))
                nc.vector.tensor_tensor_reduce(out=u_ring[:, c % U_RING, :], in0=u_ring[:, c % U_RING, :], in1=hn[:, :],
                                               scale=1.0, scalar=0.0, op0=ALU.mult, op1=ALU.add,
                                               accum_out=hid[:, par, c:c + 1]).then_inc(dot_done, 1)

            def dots(n, par, g0):
                for c in range(g0, g0 + COLS):
                    dot(n, par, c)

            def coefs(n, par, g0):
                dve.wait_ge(gelu_done, GRP * n + g0 // COLS + 1)
                nc.vector.tensor_tensor(out=coef[:, par, g0:g0 + COLS], in0=gel[:, par, g0:g0 + COLS],
                                        in1=gate[:, par, g0:g0 + COLS], op=ALU.mult).then_inc(coef_done, 1)

            def add_row(n, par, c):
                dve.wait_ge(v_in[c % V_RING], 16 * (TOPK // V_RING) * n + 16 * (c // V_RING + 1))
                dve.wait_ge(coef_done, GRP * n + c // COLS + 1)
                if n or c:
                    dve.wait_ge(v_used, TOPK * n + c)
                ht = h[:, n // PH, :]
                nc.vector.scalar_tensor_tensor(out=ht, in0=v_ring[:, c % V_RING, :], scalar=coef[:, par, c:c + 1], in1=ht,
                                               op0=ALU.mult, op1=ALU.add).then_inc(v_used, 1)

            def hn_tile(t):
                ht = h[:, t, :] if isinstance(t, int) else h[:, bass.ds(t, 1), :].rearrange("p a n -> p (a n)")
                rt = rstd2[:, t:t + 1] if isinstance(t, int) else rstd2[:, bass.ds(t, 1)]
                nc.vector.scalar_tensor_tensor(out=hn[:, :], in0=ht, scalar=rt, in1=g2b[:, :], op0=ALU.mult, op1=ALU.mult).then_inc(hn_ready, 1)
                dve.wait_ge(hn_ready, t + 1)

            def fin_tile(t):
                dve.wait_ge(v_used, PH * TOPK * (t + 1))
                dve.nop(nofuse=True)
                dve.wait_ge(out_done, 16 * (t + 1))
                dve.nop(nofuse=True)
                for half in range(2):
                    cols = slice(half * BANK, (half + 1) * BANK)
                    ht = h[:, t, cols] if isinstance(t, int) else h[:, bass.ds(t, 1), cols].rearrange("p a n -> p (a n)")
                    nc.vector.tensor_tensor(out=fin[:, cols], in0=acc[half][:, :], in1=ht, op=ALU.add).then_inc(acc_drained, 1)
                dve.wait_ge(acc_drained, 2 * t + 2)
                nc.vector.tensor_tensor_reduce(out=xs[:, :], in0=fin[:, :], in1=fin[:, :], scale=1.0, scalar=0.0,
                                               op0=ALU.mult, op1=ALU.add, accum_out=stat[:, 6:7]).then_inc(fin_step, 1)
                dve.wait_ge(fin_root, t + 1)
                nc.vector.reciprocal(fin_inv[:, :], stat[:, 7:8]).then_inc(fin_step, 1)
                dve.wait_ge(fin_step, FIN * t + 2)
                nc.vector.scalar_tensor_tensor(out=fin[:, :], in0=fin[:, :], scalar=fin_inv[:, 0:1], in1=gfb[:, :],
                                               op0=ALU.mult, op1=ALU.mult).then_inc(fin_step, 1)

            nc.vector.memset(ones[:, :], 1.0)
            nc.vector.memset(ones_row[:, :], 1.0)
            nc.vector.memset(eps[:, :], EPS)
            nc.vector.memset(selq[:, :, :], 0.0)
            link(nc.vector.memset(caug[:, :], 0.0))
            dve.wait_ge(pool_const, 6)
            for lo in (0, HD):
                nc.vector.memset(caug[lo + 32:lo + 40, :], 1.0)
                nc.vector.tensor_copy(selq[lo:lo + FH, :, :], ident[0:FH, 0:FH].unsqueeze(2).broadcast_to([FH, FH, P]))
            nc.vector.tensor_copy(iota_f[:, :], iota_i[:, :])
            link(nc.vector.tensor_copy(dist[:, :], fin[:, 0:SEQ].bitcast(I32)))
            link(nc.vector.scalar_tensor_tensor(out=dist[:, :], in0=dist[:, :], scalar=-1.0, in1=dist[:, :], op0=ALU.mult, op1=ALU.max))
            link(nc.vector.tensor_scalar(dist[0:CHUNK, SEQ - CHUNK:SEQ], dist[0:CHUNK, SEQ - CHUNK:SEQ], BIG, None, ALU.add))
            bk = mm_wait(("gain1",))
            nc.vector.tensor_copy(g1c[:, :], bk[:, 0:KC]).then_inc(mm_drained, 1)
            dve.wait_ge(*emptied(("gain1",)))

            for p_ in BEFORE:
                piece(*p_)

            def topk_all(n, par):
                topk_first(n, par)
                topk_second(n, par)
                topk_gates(n, par)

            def next_head(n, par, grp):
                if grp == 0:
                    topk_first(n + 1, 1 - par)
                elif grp == 1:
                    topk_second(n + 1, 1 - par)
                elif grp == 3:
                    topk_gates(n + 1, 1 - par)

            topk_all(0, 0)
            for tile in range(HOSTS):
                hn_tile(tile)
                for n in range(PH * tile, PH * tile + PH):
                    par = n % 2
                    for grp in range(GRP):
                        for gap in range(GAPS):
                            if gap < COLS:
                                dot(n, par, grp * COLS + gap)
                            elif gap < 2 * COLS:
                                if gap == COLS:
                                    coefs(n, par, grp * COLS)
                                    if tile and n == PH * tile and grp == 0:
                                        fin_tile(tile - 1)
                                add_row(n, par, grp * COLS + gap - COLS)
                            elif n < PH * tile + PH - 1:
                                next_head(n, par, grp)
                            for p_ in pieces_in(n, grp, gap):
                                piece(*p_)
                topk_all(PH * tile + PH, 0)
                dve.wait_ge(*emptied(MM[-1]))
                dve.wait_ge(*emptied(next(u for u in reversed(MM) if u[0] not in ON_SCALAR)))
                for half in range(2):
                    link(nc.vector.memset(acc[half][:, :], 0.0))
            with dve.Fori(HOSTS, TILES) as t:
                hn_tile(t)
                for par in range(2):
                    for grp in range(GRP):
                        n = PH * t + par
                        dots(n, par, grp * COLS)
                        coefs(n, par, grp * COLS)
                        if par == 0 and grp == 0:
                            fin_tile(t - 1)
                        next_head(n, par, grp)
                with dve.Fori(1, PH // 2) as i:
                    for par in range(2):
                        for grp in range(GRP):
                            n = PH * t + 2 * i + par
                            dots(n, par, grp * COLS)
                            coefs(n, par, grp * COLS)
                            next_head(n, par, grp)
            fin_tile(TILES - 1)


_INS = ['x', 'norm1_g', 'w_in', 'b_f', 'lambda_q1', 'lambda_k1', 'lambda_q2', 'lambda_k2', 'subln_g', 'w_out',
        'norm2_g', 'peer_w_q', 'peer_sub_keys', 'peer_u', 'peer_v', 'final_g']


def kernel(**inputs):
    import numpy as _np
    import concourse.bacc as _bacc
    from concourse import mybir as _mybir
    from concourse.bass_utils import run_bass_kernel_spmd as _run

    nc = _bacc.Bacc("TRN2", target_bir_lowering=False, num_devices=1)
    arrays, args = {}, []
    for name in _INS:
        a = _np.ascontiguousarray(inputs[name])
        arrays[f"in_{name}_dram"] = a
        args.append(nc.dram_tensor(f"in_{name}_dram", a.shape, _mybir.dt.from_np(a.dtype), kind="ExternalInput").ap())
    shape = inputs['x'].shape
    args.append(nc.dram_tensor("out_0_dram", shape, _mybir.dt.from_np(_np.dtype('float32')), kind="ExternalOutput").ap())
    build(nc, *args)
    r = _run(nc, [arrays], core_ids=[0])
    return r.results[0]["out_0_dram"]
```

```python
import math
from contextlib import ExitStack

import concourse.bass as bass
from concourse import mybir

F32 = mybir.dt.float32
I32 = mybir.dt.int32
U32 = mybir.dt.uint32
ALU = mybir.AluOpType
ACT = mybir.ActivationFunctionType
AX = mybir.AxisListType.X

P = 128
HALF_BANK = 256
BANK = 512
EPS = 1e-6
BIG = 1e30
HUGE = 3e38
LAMBDA_INIT = 0.8 - 0.6 * math.exp(-0.3 * 0)

GROUPS = [[0], [1, 2, 3]]
HOSTS = 1
SHARE_ATTEND = [1.5, 2.2, 3.3, 4.4]
SHARE_ROWS = (3.6, 3.6)
SHARE_COLS = (1.0, 2.2)
EARLY_HEADS = 1
TURN_LAG, VALUES_LAG = 3, 4
COLS = 4
U_RING = 4
V_RING = 4
W_RING = 2
EARLY_SLABS = 16
S_RING = 6


def build(nc, x, norm1_g, w_in, b_f, lambda_q1, lambda_k1, lambda_q2, lambda_k2, subln_g, w_out,
          norm2_g, peer_w_q, peer_sub_keys, peer_u, peer_v, final_g, out):
    _, SEQ, D = x.shape
    KC = D // P
    FH = b_f.shape[1]
    HD = lambda_q1.shape[1]
    DH = subln_g.shape[1]
    NDH = D // 2 // DH
    FW = FH * HD
    TILES = SEQ // P
    PH, K1 = peer_sub_keys.shape[1], peer_sub_keys.shape[3]
    TOPK = 16
    SLAB = HALF_BANK
    CHUNK = 64
    slopes = [2.0 ** (-8.0 * (i + 1) / NDH) for i in range(NDH)]
    HEADS = TILES * PH
    max_n = P * max(len(g) for g in GROUPS)

    in_kinds = []
    for kind, base in (("qa", 0), ("ka", FW), ("va", 2 * FW),
                       ("qb", 3 * FW + FH), ("kb", 4 * FW + FH), ("vb", 5 * FW + FH)):
        for c in range(0, FW, SLAB):
            in_kinds.append((kind, base + c, c))
    slab_src = ([w_in[0][:, c:c + SLAB] for _, c, _ in in_kinds]
                + [w_out[0][r:r + BANK, c:c + BANK] for r in range(0, D, BANK) for c in range(0, D, BANK)]
                + [peer_w_q[0][:, c:c + SLAB] for c in range(0, PH * 2 * P, SLAB)])
    N_IN, N_OUT = len(in_kinds), (D // BANK) ** 2
    SLABS = len(slab_src)

    ITEMS = FH + NDH
    MAPS = FH + 2 * NDH

    def maps_of(item):
        return [item] if item < FH else [FH + 2 * (item - FH), FH + 2 * (item - FH) + 1]

    def item_of(m):
        return m if m < FH else FH + (m - FH) // 2

    def items_of(half):
        return range(FH) if half == 0 else range(FH, ITEMS)

    def steps_of(half):
        return len(items_of(half)) + VALUES_LAG

    halves = [(t, half) for g in range(len(GROUPS)) for half in range(2) for t in GROUPS[g]]
    half_no = {th: i for i, th in enumerate(halves)}
    item_list = [(t, it) for t, half in halves for it in items_of(half)]
    item_no = {ti: i for i, ti in enumerate(item_list)}
    map_list = [(t, m) for t, it in item_list for m in maps_of(it)]
    map_no = {tm: i for i, tm in enumerate(map_list)}

    def parts_of(g, s):
        return list(range(len(GROUPS[g]))) if in_rows(g, s) else [0, 1]

    def turned(g, s):
        return len(GROUPS[g]) == 1 and in_kinds[s][0] not in ("va", "vb")

    def in_rows(g, s):
        return in_kinds[s][0] in ("va", "vb") or turned(g, s)

    def projections(g, lo, hi):
        ps = []
        for s in range(lo, hi):
            ps += [("project", g, s, q) for q in parts_of(g, s)]
            if s > 0 and turned(g, s - 1) and s > lo:
                ps += [("turn", g, s - 1)]
        assert not turned(g, hi - 1)
        return ps

    def share(p):
        kind, tiles = p[0], len(GROUPS[p[1]]) if len(p) > 1 and p[0] not in ("attend", "subkeys") else 1
        if kind == "attend":
            return SHARE_ATTEND[p[1]]
        if kind == "outproj":
            return SHARE_ROWS[1]
        if kind in ("project", "query"):
            by_rows = in_rows(p[1], p[2]) if kind == "project" else tiles == 1
            if kind == "query" and by_rows and p[2] % 2:
                return 1
            return SHARE_ROWS[0] if by_rows else SHARE_COLS[0] + SHARE_COLS[1] * tiles
        return {"norm1": 4, "xT": 2, "forget": 6, "mix": 4, "mixT": 1, "turn": 1, "selq": 2, "norm2": 4, "hT": 2, "subkeys": 1,
                "lambda": 1, "keys": 1.0 * tiles}[kind]

    def woven(a, b):
        def placed(ps):
            total, at, out = sum(share(p) for p in ps), 0.0, []
            for p in ps:
                at += share(p)
                out.append((at / total, p))
            return out

        return [p for _, p in sorted(placed(a) + placed(b), key=lambda x: x[0])]

    def normed(g, t):
        return [("norm1", g, t), ("xT", g, t)]

    def pieces_of(g):
        tiles, last = GROUPS[g], GROUPS[g][-1]
        ps = normed(g, tiles[0])
        fox_in = projections(g, 0, N_IN // 2)
        values_at = fox_in.index(("project", g, 4, 0))
        ps += fox_in[:values_at] + [("forget", g)] + fox_in[values_at:values_at + 1] + [("selq", g, tiles[0])] + fox_in[values_at + 1:]
        if g == 0:
            ps += [("lambda",)]
        fox, dif = [], []
        for t in tiles:
            for s in range(steps_of(0)):
                fox += [("attend", t, 0, s)] + ([("mixT", g, t - 1, 0)] if s == 2 and t > tiles[0] else [])
                if s == FH and t < last:
                    fox += [("selq", g, t + 1)]
            for s in range(steps_of(1)):
                dif += [("attend", t, 1, s)]
                if s == 2:
                    dif += [("mixT", g, t - 1, 1)] if t > tiles[0] else [("mixT", g, last, 0)]
            dif += [("mix", g, t)]
        ps += woven(fox, projections(g, N_IN // 2, N_IN))
        ps += woven(dif, [("outproj", g, s, t) for s in range(N_OUT // 2) for t in tiles])
        if g == 0:
            ps += [("subkeys", i) for i in range(PH // 4)]
        for s in range(N_OUT // 2, N_OUT):
            for t in tiles:
                if s == N_OUT // 2 and t == last:
                    ps += [("mixT", g, t, 1)]
                ps += [("outproj", g, s, t)]
                if s == N_OUT - 1 and t == tiles[0]:
                    ps += [("norm2", g, t)]
        if g == 0:
            ps += [("subkeys", i) for i in range(PH // 4, PH // 2)]
        ps += [("hT", g, tiles[0])]
        for t in tiles[1:]:
            ps += [("norm2", g, t), ("hT", g, t)]
        queries = []
        for hd in range(PH):
            queries += [("query", g, 2 * hd)]
            if hd > 0:
                queries += [("keys", g, hd - 1)]
            queries += [("query", g, 2 * hd + 1)]
            if g + 1 < len(GROUPS) and hd in range(PH // 2, PH // 2 + len(GROUPS[g + 1]) - 1):
                queries += normed(g + 1, GROUPS[g + 1][hd - PH // 2 + 1])
        return ps + queries + [("keys", g, PH - 1)]

    GRP = TOPK // COLS
    SLOTS = HOSTS * PH * GRP
    GAPS = 2 * COLS + 1
    first_pieces = pieces_of(0)
    cut_at = first_pieces.index(("keys", 0, EARLY_HEADS - 1)) + 1
    BEFORE, later = first_pieces[:cut_at], first_pieces[cut_at:] + pieces_of(1)

    AFTER = [[] for _ in range(SLOTS * GAPS)]
    total, at = sum(share(p) for p in later), 0.0
    for p in later:
        k = min(SLOTS * GAPS - 1, int(at / total * SLOTS * GAPS))
        searched = p[2] + p[1] * PH if p[0] == "keys" and (p[1] == 0 or p[2] == 0) else None
        assert searched is None or k < (searched - 1) * GRP * GAPS + 2 * COLS, p
        AFTER[k].append(p)
        at += share(p)
    ORDER = BEFORE + [p for ps in AFTER for p in ps]

    MM = [("gain1",)]
    slab_order, slab_last_use = [], {}
    for p in ORDER:
        kind, slab_used = p[0], None
        if kind == "mixT":
            MM.append(("mixT", p[2], p[3]))
        elif kind in ("xT", "hT"):
            MM += [(kind, p[2], hf) for hf in range(2)]
        elif kind in ("forget", "lambda", "query", "subkeys"):
            MM.append(p)
        elif kind == "turn":
            MM.append(p)
        elif kind == "project":
            MM.append(p)
            slab_used = (p[1], p[2])
        elif kind == "outproj":
            MM.append(p)
            slab_used = (p[1], N_IN + p[2])
        elif kind == "keys":
            MM += [("keys", p[2], t) for t in GROUPS[p[1]]]
        if kind == "query" and (len(GROUPS[p[1]]) > 1 or p[2] % 2 == 0):
            slab_used = (p[1], N_IN + N_OUT + p[2] // 2)
        if slab_used is not None:
            if slab_used not in slab_last_use:
                slab_order.append(slab_used)
            slab_last_use[slab_used] = len(MM) - 1
    mm_no = {name: i for i, name in enumerate(MM)}

    xs_no, xs_prev, reader = {}, {}, None
    for p in ORDER:
        if p[0] in ("norm1", "mix", "norm2"):
            kind, t = p[0], p[2]
            xs_no[(kind, t)] = len(xs_no) + 1
            xs_prev[(kind, t)] = reader
            if kind != "mix":
                reader = ("xT" if kind == "norm1" else "hT", t, 1)

    squares = {name: i + 1 for i, name in enumerate(n for n in xs_no if n[0] != "mix")}

    def mm_done(name):
        return mm_no[name] + 1

    ON_SCALAR = ("project", "turn", "mixT", "hT", "subkeys", "query", "keys")

    with ExitStack() as ctx:
        def sb(name, shape, dt=F32):
            return ctx.enter_context(nc.sbuf_tensor(name, shape, dt))

        def sem(name):
            return ctx.enter_context(nc.semaphore(name))

        h = sb("h", [P, TILES, D])
        actT = sb("actT", [P, KC, max_n])
        store = sb("store", [P, PH * 2 * K1 + KC * max_n + KC * SEQ])
        key_sc = store[:, 0:HEADS * 2 * K1].rearrange("p (h k) -> p h k", k=2 * K1)
        q_at = PH * 2 * K1
        k_at = q_at + KC * max_n
        assert k_at + KC * SEQ >= HEADS * 2 * K1
        qT = store[:, q_at:k_at].rearrange("p (c n) -> p c n", c=KC)
        kv_t = store[:, k_at:k_at + KC * SEQ].rearrange("p (c n) -> p c n", c=KC)
        v_all = sb("v_all", [P, TILES, D])
        qyT = sb("qyT", [P, 3, max_n])
        w_ring = sb("w_ring", [P, W_RING, KC, SLAB])
        xs = sb("xs", [P, D])
        hn = sb("hn", [P, D])
        fin = sb("fin", [P, D])
        u_ring = sb("u_ring", [P, U_RING, D])
        v_ring = sb("v_ring", [P, V_RING, D])
        v_slabs = v_ring[:, :, :].rearrange("p a b -> p (a b)").rearrange("p (s c n) -> p s c n", s=W_RING, c=KC)
        sk_raw = u_ring[:, :, :].rearrange("p a b -> p (a b)")[:, 0:2 * PH * P].rearrange("p (c n) -> p c n", c=2 * PH)
        s_maps = sb("s_maps", [P, S_RING, SEQ])
        pT = sb("pT", [P, 2, SEQ])
        mix = sb("mix", [P, D])
        staged = mix[:, FW:D].rearrange("p (a n) -> p a n", a=2)
        causal = sb("causal", [P, SEQ])
        dist = sb("dist", [P, SEQ])
        g2b = sb("g2b", [P, D])
        gfb = sb("gfb", [P, D])
        g1r = sb("g1r", [KC, P])
        g1c = sb("g1c", [P, KC])
        sub_c = sb("sub_c", [P, 1])
        subkT = sb("subkT", [P, 2 * PH, K1])
        ident = sb("ident", [P, P])
        diag = sb("diag", [P, COLS, P])
        wf = sb("wf", [P, KC, FH])
        bf = sb("bf", [FH, 1])
        c_all = sb("c_all", [FH, SEQ])
        z_f = sb("z_f", [FH, max_n])
        e_f = sb("e_f", [FH, max_n])
        selq = sb("selq", [P, FH, P])
        caug = sb("caug", [P, SEQ])
        ones = sb("ones", [P, 1])
        eps = sb("eps", [P, 1])
        ones_row = sb("ones_row", [1, P])
        lam_in = sb("lam_in", [1, 4, HD])
        lam_s = sb("lam_s", [1, 8])
        neglam = sb("neglam", [P, 1])
        stat = sb("stat", [P, 16])
        rstd2 = sb("rstd2", [P, TILES])
        negmax = sb("negmax", [P, MAPS])
        rowsum = sb("rowsum", [P, MAPS])
        rinv = sb("rinv", [P, MAPS])
        iota_i = sb("iota_i", [P, 16], I32)
        iota_f = sb("iota_f", [P, 16])
        tk_v = sb("tk_v", [P, 2, TOPK])
        tk_i = sb("tk_i", [P, 2, TOPK], U32)
        tk_if = sb("tk_if", [P, 2, TOPK])
        tk_s = sb("tk_s", [P, 2, K1])
        tk_w = sb("tk_w", [P, 2, K1])
        cand = sb("cand", [P, TOPK, TOPK])
        top_v = sb("top_v", [P, TOPK])
        top_p = sb("top_p", [P, TOPK], U32)
        top_hl = sb("top_hl", [P, 2, TOPK], U32)
        top_hlf = sb("top_hlf", [P, 2, TOPK])
        onehot = sb("onehot", [P, 2 * TOPK, TOPK])
        cand_w = onehot[:, 0:TOPK, :]
        picked = sb("picked", [P, 2, TOPK])
        eidx = [sb(f"eidx{i}", [P, TOPK], I32) for i in range(2)]
        gneg = sb("gneg", [P, 1])
        gexp = sb("gexp", [P, TOPK])
        fin_inv = sb("fin_inv", [P, 1])
        gsum = sb("gsum", [P, 1])
        gate = sb("gate", [P, 2, TOPK])
        hid = sb("hid", [P, 2, TOPK])
        gel = sb("gel", [P, 2, TOPK])
        coef = sb("coef", [P, 2, TOPK])

        def bank(name):
            return ctx.enter_context(nc.psum_tensor(name, [P, BANK], F32))

        acc = [bank("acc0"), bank("acc1")]
        mm = [bank("mm0"), bank("mm1"), acc[0]]
        sc_b = [bank("sc0"), bank("sc1"), acc[1]]
        tr_b = bank("tr")
        o_b = bank("o")

        x_in = [sem(f"x_in{t}") for t in range(TILES)]
        consts_in = sem("consts_in")
        g1_in = sem("g1_in")
        gains_in = sem("gains_in")
        slab_in = [sem(f"slab_in{i}") for i in range(2 * W_RING)]
        pool_const = sem("pool_const")
        dve_const = sem("dve_const")
        mm_full = sem("mm_full")
        mm_copied = sem("mm_copied")
        mm_drained = sem("mm_drained")
        xs_ready = sem("xs_ready")
        act_norm = sem("act_norm")
        dve_chain = sem("dve_chain")
        eps_ready = sem("eps_ready")
        squared = sem("squared")
        norm_ask = sem("norm_ask")
        selq_ready = sem("selq_ready")
        sc_full, sc_drained = sem("sc_full"), sem("sc_drained")
        exp_done = sem("exp_done")
        comb_done = sem("comb_done")
        tr_full, tr_drained = sem("tr_full"), sem("tr_drained")
        pv_done = sem("pv_done")
        o_drained = sem("o_drained")
        topk_step = sem("topk_step")
        gexp_done = sem("gexp_done")
        u_in = [sem(f"u_in{i}") for i in range(U_RING)]
        v_in = [sem(f"v_in{i}") for i in range(V_RING)]
        dot_done = sem("dot_done")
        gelu_done = sem("gelu_done")
        coef_done = sem("coef_done")
        diag_done = sem("diag_done")
        v_used = sem("v_used")
        acc_drained = sem("acc_drained")
        fin_step = sem("fin_step")
        fin_root = sem("fin_root")
        hn_ready = sem("hn_ready")
        out_done = sem("out_done")

        def emptied(name):
            scalar = name[0] in ON_SCALAR
            count = sum((u[0] in ON_SCALAR) == scalar for u in MM[:mm_no[name] + 1])
            return (mm_copied if scalar else mm_drained), count

        def slab_place(n):
            if n < EARLY_SLABS:
                return n % (2 * W_RING), n - 2 * W_RING
            return n % W_RING, n - (2 * W_RING if n < EARLY_SLABS + W_RING else W_RING)

        def slab_count(n):
            return 1 + (slab_count(slab_place(n)[1]) if slab_place(n)[1] >= 0 else 0)

        def slab_view(n, sl):
            place = slab_place(n)[0]
            w = w_ring[:, place, :, :] if place < W_RING else v_slabs[:, place - W_RING, :, :]
            if N_IN <= sl < N_IN + N_OUT:
                return w.rearrange("p c n -> p (c n)").rearrange("p (c n) -> p c n", n=BANK)
            return w

        def pieces_in(n, grp, gap):
            return AFTER[(n * GRP + grp) * GAPS + gap]

        TK = 29
        TK_IDX = 26
        TK_NEG = 27
        PARTS = 9
        FIN = 3

        assert PARTS == GAPS
        block = ctx.enter_context(nc.Block())

        @block.sync
        def _(sp):
            sp.dma_start(h[:, 0, :], x[0, 0:P, :]).then_inc(x_in[0], 16)
            sp.dma_start(g1r[:, :], norm1_g[0].rearrange("(c p) -> c p", p=P)).then_inc(g1_in, 16)
            def load_slab(n):
                g, sl = slab_order[n]
                place, before = slab_place(n)
                if before >= 0:
                    sp.wait_ge(mm_full, slab_last_use[slab_order[before]] + 1)
                sp.dma_start(slab_view(n, sl),
                             slab_src[sl].rearrange("(c p) n -> p c n", p=P)).then_inc(slab_in[place], 16)

            for n in range(2 * W_RING):
                load_slab(n)
            sp.dma_start(sk_raw, peer_sub_keys[0].rearrange("h s k d -> k (h s) d")).then_inc(consts_in, 16)
            for i, v in enumerate((lambda_q1, lambda_q2, lambda_k1, lambda_k2)):
                sp.dma_start(lam_in[:, i, :], v).then_inc(consts_in, 16)
            sp.dma_start(sub_c[:, :], subln_g.rearrange("a p -> p a")).then_inc(consts_in, 16)
            sp.dma_start(wf[:, :, :], w_in[0][:, 3 * FW:3 * FW + FH].rearrange("(c p) n -> p c n", p=P)).then_inc(consts_in, 16)
            sp.dma_start(bf[:, :], b_f.rearrange("a p -> p a")).then_inc(consts_in, 16)

            sp.dma_start(g2b[:, :], norm2_g.broadcast_to([P, D])).then_inc(gains_in, 16)
            sp.dma_start(gfb[:, :], final_g.rearrange("(a n) -> a n", a=1).broadcast_to([P, D])).then_inc(out_done, 16)
            for t in range(1, TILES):
                sp.dma_start(h[:, t, :], x[0, t * P:(t + 1) * P, :]).then_inc(x_in[t], 16)
            for n in range(2 * W_RING, len(slab_order)):
                load_slab(n)

            with sp.Fori(0, TILES) as t:
                sp.wait_ge(fin_step, FIN * t + FIN)
                sp.dma_start(out[0, bass.ds(t * P, P), :], fin[:, :]).then_inc(out_done, 16)
            sp.wait_ge(out_done, 16 * (TILES + 1))

        @block.gpsimd
        def _(pool):
            nc.gpsimd.memset(ident[:, :], 0.0).then_inc(pool_const, 1)
            nc.gpsimd.memset(causal[:, :], 0.0).then_inc(pool_const, 1)
            nc.gpsimd.iota(fin[:, 0:SEQ].bitcast(I32), pattern=[[1, SEQ]], base=-(SEQ - P), channel_multiplier=-1).then_inc(pool_const, 1)
            nc.gpsimd.iota(iota_i[:, :], pattern=[[1, TOPK]], base=0, channel_multiplier=0).then_inc(pool_const, 1)
            pool.wait_ge(pool_const, 4)
            nc.gpsimd.affine_select(out=ident[:, :], in_=ident[:, :], compare_op=ALU.not_equal, fill=1.0,
                                    base=0, pattern=[[-1, P]], channel_multiplier=1).then_inc(pool_const, 1)
            nc.gpsimd.affine_select(out=causal[:, SEQ - P:SEQ], in_=causal[:, SEQ - P:SEQ], compare_op=ALU.is_ge, fill=-BIG,
                                    base=0, pattern=[[-1, P]], channel_multiplier=1).then_inc(pool_const, 1)

            def gather_u(n, par, c):
                if not (isinstance(n, int) and n == 0 and c < U_RING):
                    pool.wait_ge(dot_done, TOPK * n + c + 1 - U_RING)
                    pool.nop(nofuse=True)
                nc.gpsimd.indirect_dma_start(
                    out=u_ring[:, c % U_RING, :], out_offset=None, in_=peer_u[0],
                    in_offset=bass.IndirectOffsetOnAxis(ap=eidx[par][:, c:c + 1], axis=0)).then_inc(u_in[c % U_RING], 16)

            def gather_v(n, par, c):
                if not (isinstance(n, int) and n == 0 and c < V_RING):
                    pool.wait_ge(v_used, TOPK * n + c + 1 - V_RING)
                    pool.nop(nofuse=True)
                nc.gpsimd.indirect_dma_start(
                    out=v_ring[:, c % V_RING, :], out_offset=None, in_=peer_v[0],
                    in_offset=bass.IndirectOffsetOnAxis(ap=eidx[par][:, c:c + 1], axis=0)).then_inc(v_in[c % V_RING], 16)

            def numbers_of(n):
                pool.wait_ge(topk_step, TK * n + TK_IDX)
                pool.nop(nofuse=True)

            def gathers(n, par, last):
                for c in range(TOPK):
                    ahead = c + COLS
                    if ahead < TOPK:
                        gather_u(n, par, ahead)
                    elif not last:
                        if ahead == TOPK:
                            numbers_of(n + 1)
                        gather_u(n + 1, 1 - par, ahead - TOPK)
                    gather_v(n, par, c)

            numbers_of(0)
            for c in range(COLS):
                gather_u(0, 0, c)
            for n in range(PH * HOSTS):
                gathers(n, n % 2, False)
            with pool.Fori(PH * HOSTS // 2, HEADS // 2 - 1) as i:
                for par in range(2):
                    gathers(2 * i + par, par, False)
            for par in range(2):
                gathers(HEADS - 2 + par, par, par == 1)

        @block.tensor
        def _(pe):
            def mm_bank(name):
                n = mm_no[name]
                if n >= len(mm):
                    pe.wait_ge(*emptied(MM[n - len(mm)]))
                return mm[n % len(mm)]

            def transposes(name, src):
                b = mm_bank(name)
                for j in range(4):
                    last = nc.tensor.transpose(b[:, j * P:(j + 1) * P], src(j), ident[:, :])
                last.then_inc(mm_full, 1)

            def slab(g, sl):
                n = slab_order.index((g, sl))
                pe.wait_ge(slab_in[slab_place(n)[0]], 16 * slab_count(n))
                return slab_view(n, sl)

            def rows_out(name, j, w):
                bk = mm_bank(name)
                for c in range(KC):
                    last = nc.tensor.matmul(bk[:, 0:SLAB], actT[:, c, j * P:(j + 1) * P], w[:, c, :],
                                            start=(c == 0), stop=(c == KC - 1))
                last.then_inc(mm_full, 1)

            def cols_out(name, n, w, q):
                bk = mm_bank(name)
                for c in range(KC):
                    last = nc.tensor.matmul(bk[:, 0:n], w[:, c, q * P:(q + 1) * P], actT[:, c, 0:n],
                                            start=(c == 0), stop=(c == KC - 1))
                last.then_inc(mm_full, 1)

            def turn(name, at):
                bk = mm_bank(name)
                for q in range(2):
                    last = nc.tensor.transpose(bk[:, q * P:(q + 1) * P], staged[:, at, q * P:(q + 1) * P], ident[:, :])
                last.then_inc(mm_full, 1)

            def piece(kind, *p):
                if kind == "xT":
                    pe.wait_ge(xs_ready, xs_no[("norm1", p[1])])
                    for hf in range(2):
                        transposes(("xT", p[1], hf), lambda j: xs[:, (4 * hf + j) * P:(4 * hf + j + 1) * P])
                elif kind == "project":
                    g, sl, q = p
                    w = slab(g, sl)
                    pe.wait_ge(*emptied(("xT", GROUPS[g][0], 1)))
                    if in_rows(g, sl):
                        rows_out((kind, *p), q, w)
                    else:
                        cols_out((kind, *p), P * len(GROUPS[g]), w, q)
                elif kind == "turn":
                    g, sl = p
                    pe.wait_ge(*emptied(("project", g, sl, 0)))
                    turn((kind, *p), sl % 2)
                elif kind == "forget":
                    n = P * len(GROUPS[p[0]])
                    pe.wait_ge(consts_in, 16 * 8)
                    bk = mm_bank((kind, *p))
                    for c in range(KC):
                        last = nc.tensor.matmul(bk[0:FH, 0:n], wf[:, c, :], actT[:, c, 0:n], start=(c == 0), stop=(c == KC - 1))
                    last.then_inc(mm_full, 1)
                elif kind == "lambda":
                    pe.wait_ge(dve_const, 1)
                    nc.tensor.matmul(mm_bank(("lambda",))[:, 0:1], ones_row[:, :], lam_s[0:1, 4:5],
                                     start=True, stop=True).then_inc(mm_full, 1)
                elif kind == "subkeys":
                    i, = p
                    transposes(("subkeys", i), lambda j: sk_raw[:, 4 * i + j, :])
                elif kind == "attend":
                    attend(*p)
                elif kind == "mixT":
                    g, t, hf = p
                    if hf == 0:
                        pe.wait_ge(o_drained, half_no[(t, 0)] + 1)
                    else:
                        pe.wait_ge(xs_ready, xs_no[("mix", t)])
                    transposes(("mixT", t, hf), lambda j: mix[:, (4 * hf + j) * P:(4 * hf + j + 1) * P])
                elif kind == "outproj":
                    g, sl, t = p
                    w = slab(g, N_IN + sl)
                    hf = sl * 2 // N_OUT
                    pe.wait_ge(*emptied(("mixT", t, hf)))
                    bk, j = mm_bank((kind, *p)), GROUPS[g].index(t)
                    for c in range(KC // 2):
                        last = nc.tensor.matmul(bk[:, :], qT[:, KC // 2 * hf + c, j * P:(j + 1) * P], w[:, c, :],
                                                start=(c == 0), stop=(c == KC // 2 - 1))
                    last.then_inc(mm_full, 1)
                elif kind == "hT":
                    pe.wait_ge(xs_ready, xs_no[("norm2", p[1])])
                    for hf in range(2):
                        transposes(("hT", p[1], hf), lambda j: xs[:, (4 * hf + j) * P:(4 * hf + j + 1) * P])
                elif kind == "query":
                    g, c2 = p
                    pe.wait_ge(*emptied(("hT", GROUPS[g][-1], 1)))
                    if len(GROUPS[g]) > 1:
                        cols_out((kind, *p), P * len(GROUPS[g]), slab(g, N_IN + N_OUT + c2 // 2), c2 % 2)
                    elif c2 % 2 == 0:
                        rows_out((kind, *p), 0, slab(g, N_IN + N_OUT + c2 // 2))
                    else:
                        pe.wait_ge(*emptied(("query", g, c2 - 1)))
                        turn((kind, *p), c2 // 2 % 2)
                elif kind == "keys":
                    g, hd = p
                    pe.wait_ge(*emptied(("query", g, 2 * hd + 1)))
                    for j, t in enumerate(GROUPS[g]):
                        bk = mm_bank(("keys", hd, t))
                        for sd in range(2):
                            c2 = 2 * hd + sd
                            last = nc.tensor.matmul(bk[:, sd * K1:(sd + 1) * K1], qyT[:, c2 % 3, j * P:(j + 1) * P], subkT[:, c2, :],
                                                    start=True, stop=True)
                        last.then_inc(mm_full, 1)

            def attend(t, half, step):
                nk = P * (t + 1)
                g = next(i for i, ts in enumerate(GROUPS) if t in ts)
                j = GROUPS[g].index(t)
                items = items_of(half)
                if step == 0:
                    pe.wait_ge(*emptied(("project", g, N_IN // 2 * (half + 1) - 1, len(GROUPS[g]) - 1)))
                    if half == 0:
                        pe.wait_ge(selq_ready, 2 * (t + 1))
                it = items[0] + step
                if it in items:
                    for m in maps_of(it):
                        k = map_no[(t, m)]
                        if k >= len(sc_b):
                            pe.wait_ge(sc_drained, k + 1 - len(sc_b))
                        bk = sc_b[k % len(sc_b)]
                        if m < FH:
                            lo, ch = HD * (m % 2), m // 2
                        else:
                            lo, ch = HD * ((m - FH) % 2), KC // 2 + (m - FH) // 2
                        mo = nc.tensor.matmul(bk[:, 0:nk], qT[lo:lo + HD, ch, j * P:(j + 1) * P], kv_t[lo:lo + HD, ch, 0:nk],
                                              start=True, stop=(m >= FH))
                        if m < FH:
                            mo = nc.tensor.matmul(bk[:, 0:nk], selq[lo:lo + 40, m, :], caug[lo:lo + 40, 0:nk], start=False, stop=True)
                        mo.then_inc(sc_full, 1)
                it = items[0] + step - TURN_LAG
                if it in items:
                    k = item_no[(t, it)]
                    if it < FH:
                        pe.wait_ge(exp_done, map_no[(t, it)] + 1)
                    else:
                        pe.wait_ge(comb_done, NDH * t + it - FH + 1)
                    if k >= 1:
                        pe.wait_ge(tr_drained, k)
                    slot = map_no[(t, maps_of(it)[0])] % S_RING
                    for q in range(t + 1):
                        last = nc.tensor.transpose(tr_b[:, q * P:(q + 1) * P], s_maps[:, slot, q * P:(q + 1) * P], ident[:, :])
                    last.then_inc(tr_full, 1)
                it = items[0] + step - VALUES_LAG
                if it in items:
                    k = item_no[(t, it)]
                    pe.wait_ge(tr_drained, k + 1)
                    if it == items[0] and half_no[(t, half)] > 0:
                        pe.wait_ge(o_drained, half_no[(t, half)])
                    w = HD if it < FH else DH
                    col = HD * it if it < FH else DH * (it - FH)
                    vcol = col if it < FH else FW + col
                    for q in range(t + 1):
                        last = nc.tensor.matmul(o_b[:, col:col + w], pT[:, k % 2, q * P:(q + 1) * P], v_all[:, q, vcol:vcol + w],
                                                start=(q == 0), stop=(q == t))
                    last.then_inc(pv_done, 1)

            def peer_group(n, g0, starts, emptied):
                for c in range(g0, g0 + COLS):
                    if c == 0 and emptied is not None:
                        pe.wait_ge(acc_drained, emptied)
                    pe.wait_ge(v_in[c % V_RING], 16 * (TOPK // V_RING) * n + 16 * (c // V_RING + 1))
                    pe.wait_ge(diag_done, TOPK * (n - PH * HOSTS) + c + 1)
                    for half in range(2):
                        last = nc.tensor.matmul(acc[half][:, :], diag[:, c % COLS, :], v_ring[:, c % V_RING, half * BANK:(half + 1) * BANK],
                                                start=(starts and c == 0), stop=False, skip_group_check=True)
                    last.then_inc(v_used, 1)

            pe.wait_ge(pool_const, 6)
            pe.wait_ge(g1_in, 16)
            nc.tensor.transpose(mm_bank(("gain1",))[:, 0:KC], g1r[:, :], ident[0:KC, 0:KC]).then_inc(mm_full, 1)
            for p_ in BEFORE:
                piece(*p_)
            for tile in range(HOSTS):
                for n in range(PH * tile, PH * tile + PH):
                    for grp in range(GRP):
                        for gap in range(GAPS):
                            for p_ in pieces_in(n, grp, gap):
                                piece(*p_)
            with pe.Fori(HOSTS, TILES) as t:
                for par in range(2):
                    for grp in range(GRP):
                        peer_group(PH * t + par, grp * COLS, par == 0, 2 * t if par == 0 else None)
                with pe.Fori(1, PH // 2) as i:
                    for par in range(2):
                        for grp in range(GRP):
                            peer_group(PH * t + 2 * i + par, grp * COLS, False, None)

        @block.scalar
        def _(act):
            asked = [0]
            given = [0]

            def mm_wait(name):
                act.wait_ge(mm_full, mm_done(name))
                return mm[mm_no[name] % len(mm)]

            def four(b):
                return b[:, :].rearrange("p (c n) -> p c n", c=4)

            def root(dst, src, scale, count=None):
                asked[0] += 1
                given[0] += 1
                act.wait_ge(norm_ask, asked[0])
                nc.scalar.activation(dst, src, ACT.Sqrt, scale=scale, bias=eps[:, 0:1]).then_inc(act_norm, 1)

            def norm_rows(kind, t, st):
                if xs_prev[(kind, t)] is not None:
                    act.wait_ge(mm_full, mm_done(xs_prev[(kind, t)]))
                if xs_no[(kind, t)] > 1:
                    act.wait_ge(xs_ready, xs_no[(kind, t)] - 1)
                nc.scalar.activation(xs[:, :], h[:, t, :], ACT.Square, accum_out=stat[:, st:st + 1]).then_inc(squared, 1)
                act.wait_ge(squared, squares[(kind, t)])
                nc.scalar.activation(stat[:, st + 1:st + 2], stat[:, st:st + 1], ACT.Sqrt, scale=1.0 / D,
                                     bias=eps[:, 0:1]).then_inc(act_norm, 1)
                given[0] += 1

            def query_scale(knd, ch):
                return HD ** -0.5 if knd == "qa" else -(HD ** -0.5) / slopes[ch - KC // 2]

            def piece(kind, *p):
                if kind == "norm1":
                    act.wait_ge(x_in[p[1]], 16)
                    norm_rows(kind, p[1], 0)
                elif kind == "norm2":
                    act.wait_ge(*emptied(("outproj", p[0], N_OUT - 1, p[1])))
                    norm_rows(kind, p[1], 4)
                elif kind == "mix":
                    root(stat[:, 12:12 + NDH], stat[:, 8:8 + NDH], 1.0 / DH)
                elif kind == "project":
                    g, sl, q = p
                    n = P * len(GROUPS[g])
                    knd, _, col = in_kinds[sl]
                    bk = mm_wait((kind, *p))
                    if turned(g, sl):
                        nc.scalar.activation(staged[:, sl % 2, :], bk[:, 0:SLAB], ACT.Copy).then_inc(mm_copied, 1)
                    elif knd in ("va", "vb"):
                        col += FW if knd == "vb" else 0
                        nc.scalar.activation(v_all[:, GROUPS[g][q], col:col + SLAB], bk[:, 0:SLAB], ACT.Copy).then_inc(mm_copied, 1)
                    else:
                        ch = col // P + q + (KC // 2 if knd in ("qb", "kb") else 0)
                        if knd in ("ka", "kb"):
                            t0 = GROUPS[g][0] * P
                            nc.scalar.activation(kv_t[:, ch, t0:t0 + n], bk[:, 0:n], ACT.Copy).then_inc(mm_copied, 1)
                        else:
                            nc.scalar.activation(qT[:, ch, 0:n], bk[:, 0:n], ACT.Copy, scale=query_scale(knd, ch)).then_inc(mm_copied, 1)
                elif kind == "turn":
                    g, sl = p
                    knd, _, col = in_kinds[sl]
                    bk = mm_wait((kind, *p))
                    for q in range(2):
                        ch = col // P + q + (KC // 2 if knd in ("qb", "kb") else 0)
                        if knd in ("ka", "kb"):
                            last = nc.scalar.activation(kv_t[:, ch, 0:P], bk[:, q * P:(q + 1) * P], ACT.Copy)
                        else:
                            last = nc.scalar.activation(qT[:, ch, 0:P], bk[:, q * P:(q + 1) * P], ACT.Copy, scale=query_scale(knd, ch))
                    last.then_inc(mm_copied, 1)
                elif kind == "subkeys":
                    i, = p
                    bk = mm_wait(("subkeys", i))
                    nc.scalar.activation(subkT[:, 4 * i:4 * i + 4, :], four(bk), ACT.Copy).then_inc(mm_copied, 1)
                elif kind == "mixT":
                    g, t, hf = p
                    j = GROUPS[g].index(t)
                    bk = mm_wait(("mixT", t, hf))
                    if hf == 0:
                        nc.scalar.activation(qT[:, 0:4, j * P:(j + 1) * P], four(bk), ACT.Copy).then_inc(mm_copied, 1)
                    else:
                        act.wait_ge(dve_const, 1)
                        nc.scalar.activation(qT[:, 4:8, j * P:(j + 1) * P], four(bk), ACT.Copy, scale=sub_c[:, 0:1]).then_inc(mm_copied, 1)
                elif kind == "hT":
                    g, t = p
                    j = GROUPS[g].index(t)
                    for hf in range(2):
                        bk = mm_wait(("hT", t, hf))
                        nc.scalar.activation(actT[:, 4 * hf:4 * hf + 4, j * P:(j + 1) * P], four(bk), ACT.Copy).then_inc(mm_copied, 1)
                elif kind == "query":
                    g, c2 = p
                    n = P * len(GROUPS[g])
                    bk = mm_wait((kind, *p))
                    if len(GROUPS[g]) > 1:
                        nc.scalar.activation(qyT[:, c2 % 3, 0:n], bk[:, 0:n], ACT.Copy).then_inc(mm_copied, 1)
                    elif c2 % 2 == 0:
                        nc.scalar.activation(staged[:, c2 // 2 % 2, :], bk[:, 0:SLAB], ACT.Copy).then_inc(mm_copied, 1)
                    else:
                        for q in range(2):
                            last = nc.scalar.activation(qyT[:, (c2 - 1 + q) % 3, 0:n], bk[:, q * P:(q + 1) * P], ACT.Copy)
                        last.then_inc(mm_copied, 1)
                elif kind == "keys":
                    g, hd = p
                    for t in GROUPS[g]:
                        bk = mm_wait(("keys", hd, t))
                        nc.scalar.activation(key_sc[:, PH * t + hd, :], bk[:, 0:2 * K1], ACT.Copy).then_inc(mm_copied, 1)
                elif kind == "lambda":
                    asked[0] += 1
                    given[0] += 1
                    act.wait_ge(norm_ask, asked[0])
                    nc.scalar.activation(lam_s[0:1, 2:4], lam_s[0:1, 0:2], ACT.Exp).then_inc(act_norm, 1)
                elif kind == "forget":
                    n = P * len(GROUPS[p[0]])
                    asked[0] += 1
                    act.wait_ge(norm_ask, asked[0])
                    nc.scalar.activation(e_f[:, 0:n], e_f[:, 0:n], ACT.Exp, scale=-1.0).then_inc(act_norm, 1)
                    given[0] += 2
                    act.wait_ge(act_norm, given[0] - 1)
                    nc.scalar.activation(e_f[:, 0:n], e_f[:, 0:n], ACT.Ln, bias=1.0).then_inc(act_norm, 1)
                elif kind == "attend":
                    t, half, step = p
                    nk = P * (t + 1)
                    items = items_of(half)
                    it = items[0] + step
                    if it in items:
                        for m in maps_of(it):
                            k = map_no[(t, m)]
                            act.wait_ge(sc_drained, k + 1)
                            s = s_maps[:, k % S_RING, 0:nk]
                            nc.scalar.activation(s, s, ACT.Exp, scale=-1.0, bias=negmax[:, m:m + 1],
                                                 accum_out=rowsum[:, m:m + 1]).then_inc(exp_done, 1)
                    it = items[0] + step - TURN_LAG
                    if it in items:
                        k = item_no[(t, it)]
                        act.wait_ge(tr_full, k + 1)
                        if k >= 2:
                            act.wait_ge(pv_done, k - 1)
                        nc.scalar.activation(pT[:, k % 2, 0:nk], tr_b[:, 0:nk], ACT.Copy).then_inc(tr_drained, 1)

            def gate_exp(n):
                act.wait_ge(topk_step, TK * n + TK_NEG)
                nc.scalar.activation(gexp[:, :], top_v[:, :], ACT.Exp, bias=gneg[:, 0:1], accum_out=gsum[:, 0:1]).then_inc(gexp_done, 1)

            def gelu(n, par, g0):
                act.wait_ge(dot_done, TOPK * n + g0 + COLS)
                nc.scalar.activation(gel[:, par, g0:g0 + COLS], hid[:, par, g0:g0 + COLS], ACT.Gelu).then_inc(gelu_done, 1)

            def peer_group(n, par, g0):
                gelu(n, par, g0)
                act.wait_ge(coef_done, GRP * n + g0 // COLS + 1)
                for c in range(COLS):
                    act.wait_ge(v_used, TOPK * n + g0 + c + 1 - COLS)
                    nc.scalar.activation(diag[:, c, :], ident[:, :], ACT.Copy,
                                         scale=coef[:, par, g0 + c:g0 + c + 1]).then_inc(diag_done, 1)

            def fin_rt(t):
                act.wait_ge(fin_step, FIN * t + 1)
                nc.scalar.activation(stat[:, 7:8], stat[:, 6:7], ACT.Sqrt, scale=1.0 / D, bias=eps[:, 0:1]).then_inc(fin_root, 1)

            act.wait_ge(eps_ready, 1)
            act.wait_ge(pool_const, 6)
            for p_ in BEFORE:
                piece(*p_)
            gate_exp(0)
            for tile in range(HOSTS):
                for n in range(PH * tile, PH * tile + PH):
                    for grp in range(GRP):
                        for gap in range(GAPS):
                            if gap == 2 * COLS - 2:
                                gelu(n, n % 2, grp * COLS)
                            for p_ in pieces_in(n, grp, gap):
                                piece(*p_)
                        if tile and n == PH * tile and grp == 0:
                            fin_rt(tile - 1)
                        if grp == 2:
                            gate_exp(n + 1)
            with act.Fori(HOSTS, TILES) as t:
                for par in range(2):
                    for grp in range(GRP):
                        peer_group(PH * t + par, par, grp * COLS)
                        if par == 0 and grp == 0:
                            fin_rt(t - 1)
                        if grp == 2:
                            gate_exp(PH * t + par + 1)
                with act.Fori(1, PH // 2) as i:
                    for par in range(2):
                        for grp in range(GRP):
                            peer_group(PH * t + 2 * i + par, par, grp * COLS)
                            if grp == 2:
                                gate_exp(PH * t + 2 * i + par + 1)
            fin_rt(TILES - 1)

        @block.vector
        def _(dve):
            chain = [0]
            rooted = [0]
            handed = [0]

            def link(ins):
                chain[0] += 1
                ins.then_inc(dve_chain, 1)
                dve.wait_ge(dve_chain, chain[0])

            def from_act(ins, steps=1):
                ins.then_inc(norm_ask, 1)
                rooted[0] += steps
                dve.wait_ge(act_norm, rooted[0])

            def mm_wait(name):
                dve.wait_ge(mm_full, mm_done(name))
                return mm[mm_no[name] % len(mm)]

            def four(b):
                return b[:, :].rearrange("p (c n) -> p c n", c=4)

            def norm_root():
                rooted[0] += 1
                dve.wait_ge(act_norm, rooted[0])

            def piece(kind, *p):
                if kind == "norm1":
                    g, t = p
                    dve.wait_ge(x_in[t], 16)
                    norm_root()
                    link(nc.vector.reciprocal(stat[:, 2:3], stat[:, 1:2]))
                    nc.vector.tensor_scalar(xs[:, :], h[:, t, :], stat[:, 2:3], None, ALU.mult).then_inc(xs_ready, 1)
                elif kind == "xT":
                    g, t = p
                    j = GROUPS[g].index(t)
                    if j == 0 and g > 0:
                        dve.wait_ge(mm_full, mm_done(("query", g - 1, 2 * PH - 1)))
                    for hf in range(2):
                        bk = mm_wait(("xT", t, hf))
                        nc.vector.tensor_tensor(out=actT[:, 4 * hf:4 * hf + 4, j * P:(j + 1) * P], in0=four(bk),
                                                in1=g1c[:, 4 * hf:4 * hf + 4].unsqueeze(2).broadcast_to([P, 4, P]),
                                                op=ALU.mult).then_inc(mm_drained, 1)
                elif kind == "forget":
                    g, = p
                    n, t0 = P * len(GROUPS[g]), P * GROUPS[g][0]
                    dve.wait_ge(consts_in, 16 * 8)
                    bk = mm_wait(("forget", g))
                    nc.vector.tensor_scalar(z_f[:, 0:n], bk[0:FH, 0:n], bf[:, 0:1], None, ALU.add).then_inc(mm_drained, 1)
                    dve.wait_ge(*emptied(("forget", g)))
                    from_act(nc.vector.scalar_tensor_tensor(out=e_f[:, 0:n], in0=z_f[:, 0:n], scalar=-1.0, in1=z_f[:, 0:n],
                                                            op0=ALU.mult, op1=ALU.max), 2)
                    link(nc.vector.scalar_tensor_tensor(out=z_f[:, 0:n], in0=z_f[:, 0:n], scalar=0.0, in1=e_f[:, 0:n],
                                                        op0=ALU.min, op1=ALU.subtract))
                    init = 0.0 if t0 == 0 else c_all[:, t0 - 1:t0]
                    link(nc.vector.tensor_tensor_scan(c_all[:, t0:t0 + n], ones[0:FH, :].broadcast_to([FH, n]), z_f[:, 0:n],
                                                      init, ALU.mult, ALU.add))
                    for lo in (0, HD):
                        link(nc.vector.tensor_scalar(caug[lo:lo + FH, t0:t0 + n], c_all[:, t0:t0 + n], -1.0, None, ALU.mult))
                elif kind == "selq":
                    g, t = p
                    if t > 0:
                        dve.wait_ge(sc_full, map_no[(t - 1, FH - 1)] + 1)
                    for lo in (0, HD):
                        nc.vector.tensor_tensor(out=selq[lo + 32:lo + 32 + FH, :, :],
                                                in0=c_all[:, t * P:(t + 1) * P].unsqueeze(1).broadcast_to([FH, FH, P]),
                                                in1=ident[0:FH, 0:FH].unsqueeze(2).broadcast_to([FH, FH, P]),
                                                op=ALU.mult).then_inc(selq_ready, 1)
                elif kind == "lambda":
                    link(nc.vector.tensor_tensor(out=lam_in[:, 0:2, :], in0=lam_in[:, 0:2, :], in1=lam_in[:, 2:4, :], op=ALU.mult))
                    from_act(nc.vector.tensor_reduce(lam_s[0:1, 0:2], lam_in[:, 0:2, :], AX, ALU.add))
                    link(nc.vector.tensor_tensor(out=lam_s[0:1, 5:6], in0=lam_s[0:1, 3:4], in1=lam_s[0:1, 2:3], op=ALU.subtract))
                    link(nc.vector.tensor_scalar(sub_c[:, :], sub_c[:, :], 1.0 - LAMBDA_INIT, None, ALU.mult))
                    nc.vector.tensor_scalar(lam_s[0:1, 4:5], lam_s[0:1, 5:6], LAMBDA_INIT, None, ALU.subtract).then_inc(dve_const, 1)
                    bk = mm_wait(("lambda",))
                    nc.vector.tensor_copy(neglam[:, :], bk[:, 0:1]).then_inc(mm_drained, 1)
                    dve.wait_ge(*emptied(("lambda",)))
                elif kind == "attend":
                    attend(*p)
                elif kind == "mix":
                    g, t = p
                    dve.wait_ge(pv_done, item_no[(t, ITEMS - 1)] + 1)
                    if t > 0:
                        dve.wait_ge(mm_full, mm_done(("mixT", t - 1, 1)))
                    nc.vector.tensor_copy(mix[:, FW:D], o_b[:, :]).then_inc(o_drained, 1)
                    dve.wait_ge(o_drained, half_no[(t, 1)] + 1)
                    if xs_prev[("mix", t)] is not None:
                        dve.wait_ge(mm_full, mm_done(xs_prev[("mix", t)]))
                    link(nc.vector.tensor_tensor(out=xs[:, 0:FW], in0=mix[:, FW:D], in1=mix[:, FW:D], op=ALU.mult))
                    from_act(nc.vector.tensor_reduce(stat[:, 8:8 + NDH], xs[:, 0:FW].rearrange("p (a n) -> p a n", a=NDH),
                                                     AX, ALU.add))
                    link(nc.vector.reciprocal(rinv[:, 0:NDH], stat[:, 12:12 + NDH]))
                    mb = mix[:, FW:D].rearrange("p (a n) -> p a n", a=NDH)
                    nc.vector.tensor_tensor(out=mb, in0=mb, in1=rinv[:, 0:NDH].unsqueeze(2).broadcast_to([P, NDH, DH]),
                                            op=ALU.mult).then_inc(xs_ready, 1)
                elif kind == "outproj":
                    g, sl, t = p
                    bk = mm_wait((kind, *p))
                    if sl >= N_OUT // 2:
                        dve.wait_ge(*emptied(("outproj", g, sl - N_OUT // 2, t)))
                    hs = h[:, t, sl % 2 * BANK:(sl % 2 + 1) * BANK]
                    nc.vector.tensor_tensor(out=hs, in0=bk[:, :], in1=hs, op=ALU.add).then_inc(mm_drained, 1)
                elif kind == "norm2":
                    g, t = p
                    dve.wait_ge(*emptied(("outproj", g, N_OUT - 1, t)))
                    norm_root()
                    if t == 0:
                        dve.wait_ge(gains_in, 16)
                    link(nc.vector.reciprocal(rstd2[:, t:t + 1], stat[:, 5:6]))
                    nc.vector.scalar_tensor_tensor(out=xs[:, :], in0=h[:, t, :], scalar=rstd2[:, t:t + 1], in1=g2b[:, :],
                                                   op0=ALU.mult, op1=ALU.mult).then_inc(xs_ready, 1)

            def attend(t, half, step):
                nk = P * (t + 1)
                items = items_of(half)
                it = items[0] + step
                if it in items:
                    for m in maps_of(it):
                        k = map_no[(t, m)]
                        dve.wait_ge(sc_full, k + 1)
                        if k >= S_RING:
                            t0, m0 = map_list[k - S_RING]
                            dve.wait_ge(tr_full, item_no[(t0, item_of(m0))] + 1)
                        strip, scale = (causal, -1.0) if m < FH else (dist, slopes[(m - FH) // 2])
                        nc.vector.tensor_tensor_reduce(out=s_maps[:, k % S_RING, 0:nk], in0=sc_b[k % len(sc_b)][:, 0:nk],
                                                       in1=strip[:, SEQ - nk:SEQ], scale=scale, scalar=HUGE,
                                                       op0=ALU.add, op1=ALU.min, accum_out=negmax[:, m:m + 1]).then_inc(sc_drained, 1)
                it = items[0] + step - 1
                if half == 1 and it in items:
                    m1, m2 = maps_of(it)
                    dve.wait_ge(exp_done, map_no[(t, m2)] + 1)
                    link(nc.vector.reciprocal(rinv[:, m1:m2 + 1], rowsum[:, m1:m2 + 1]))
                    link(nc.vector.tensor_scalar(rinv[:, m2:m2 + 1], rinv[:, m2:m2 + 1], neglam[:, 0:1], None, ALU.mult))
                    s1 = s_maps[:, map_no[(t, m1)] % S_RING, 0:nk]
                    s2 = s_maps[:, map_no[(t, m2)] % S_RING, 0:nk]
                    link(nc.vector.tensor_scalar(s2, s2, rinv[:, m2:m2 + 1], None, ALU.mult))
                    nc.vector.scalar_tensor_tensor(out=s1, in0=s1, scalar=rinv[:, m1:m1 + 1], in1=s2,
                                                   op0=ALU.mult, op1=ALU.add).then_inc(comb_done, 1)
                if half == 0 and step == steps_of(0) - 1:
                    dve.wait_ge(pv_done, item_no[(t, FH - 1)] + 1)
                    link(nc.vector.reciprocal(rinv[:, 0:FH], rowsum[:, 0:FH]))
                    if t > 0:
                        dve.wait_ge(mm_full, mm_done(("mixT", t - 1, 0)))
                    nc.vector.tensor_tensor(out=mix[:, 0:FW].rearrange("p (a n) -> p a n", a=FH),
                                            in0=o_b[:, :].rearrange("p (a n) -> p a n", a=FH),
                                            in1=rinv[:, 0:FH].unsqueeze(2).broadcast_to([P, FH, HD]),
                                            op=ALU.mult).then_inc(o_drained, 1)

            def after_topk(n, k):
                dve.wait_ge(topk_step, TK * n + k)
                dve.nop(nofuse=True)

            def topk_first(n, par):
                if isinstance(n, int):
                    dve.wait_ge(*emptied(("keys", n % PH, n // PH)))
                def after(k):
                    after_topk(n, k)

                s = key_sc[:, n, :] if isinstance(n, int) else key_sc[:, bass.ds(n % HEADS, 1), :].rearrange("p a k -> p (a k)")
                nc.vector.tensor_copy(tk_s[:, :, :].rearrange("p a k -> p (a k)"), s).then_inc(topk_step, 1)
                after(1)
                s1 = [tk_s[:, 0, :], tk_s[:, 1, :]]
                for q in range(2):
                    nc.vector.max(tk_v[:, q, 0:8], s1[q]).then_inc(topk_step, 1)
                for q in range(2):
                    after(q + 2)
                    nc.vector.match_replace(tk_w[:, q, :], tk_v[:, q, 0:8], s1[q], -HUGE).then_inc(topk_step, 1)
                for q in range(2):
                    nc.vector.max_index(tk_i[:, q, 0:8], tk_v[:, q, 0:8], s1[q]).then_inc(topk_step, 1)
                for q in range(2):
                    after(q + 4)
                    nc.vector.max(tk_v[:, q, 8:16], tk_w[:, q, :]).then_inc(topk_step, 1)
                for q in range(2):
                    after(q + 8)
                    nc.vector.max_index(tk_i[:, q, 8:16], tk_v[:, q, 8:16], tk_w[:, q, :]).then_inc(topk_step, 1)
                nc.vector.tensor_tensor(out=cand[:, :, :], in0=tk_v[:, 0, :].unsqueeze(2).broadcast_to([P, TOPK, TOPK]),
                                        in1=tk_v[:, 1, :].unsqueeze(1).broadcast_to([P, TOPK, TOPK]),
                                        op=ALU.add).then_inc(topk_step, 1)
                after(11)
                nc.vector.tensor_copy(tk_if[:, :, :], tk_i[:, :, :]).then_inc(topk_step, 1)

            def topk_second(n, par, part):
                def after(k):
                    after_topk(n, k)

                cf = cand[:, :, :].rearrange("p a b -> p (a b)")
                wf_ = cand_w[:, :, :].rearrange("p a b -> p (a b)")
                if part == 0:
                    after(12)
                    nc.vector.max(top_v[:, 0:8], cf).then_inc(topk_step, 1)
                elif part == 1:
                    after(14)
                    nc.vector.match_replace(wf_, top_v[:, 0:8], cf, -HUGE).then_inc(topk_step, 1)
                    nc.vector.max_index(top_p[:, 0:8], top_v[:, 0:8], cf).then_inc(topk_step, 1)
                elif part == 2:
                    after(15)
                    nc.vector.max(top_v[:, 8:16], wf_).then_inc(topk_step, 1)
                elif part == 3:
                    after(17)
                    nc.vector.max_index(top_p[:, 8:16], top_v[:, 8:16], wf_).then_inc(topk_step, 1)
                elif part == 4:
                    after(18)
                    nc.vector.tensor_scalar(top_hl[:, 0, :], top_p[:, :], 4, None, ALU.logical_shift_right).then_inc(topk_step, 1)
                    nc.vector.tensor_scalar(top_hl[:, 1, :], top_p[:, :], 15, None, ALU.bitwise_and).then_inc(topk_step, 1)
                elif part == 5:
                    after(20)
                    nc.vector.tensor_copy(top_hlf[:, :, :], top_hl[:, :, :]).then_inc(topk_step, 1)
                elif part == 6:
                    after(21)
                    nc.vector.tensor_tensor(out=onehot[:, :, :], in0=top_hlf[:, :, :].rearrange("p a b -> p (a b)").unsqueeze(2).broadcast_to([P, 2 * TOPK, TOPK]),
                                            in1=iota_f[:, :].unsqueeze(1).broadcast_to([P, 2 * TOPK, TOPK]),
                                            op=ALU.is_equal).then_inc(topk_step, 1)
                elif part == 7:
                    for q in range(2):
                        after(22)
                        oh = onehot[:, q * TOPK:(q + 1) * TOPK, :]
                        nc.vector.tensor_tensor(out=oh, in0=oh, in1=tk_if[:, q, :].unsqueeze(1).broadcast_to([P, TOPK, TOPK]),
                                                op=ALU.mult).then_inc(topk_step, 1)
                else:
                    after(24)
                    nc.vector.tensor_reduce(picked[:, :, :].rearrange("p a b -> p (a b)"), onehot[:, :, :], AX, ALU.add).then_inc(topk_step, 1)
                    after(25)
                    if not (isinstance(n, int) and n < 2):
                        dve.wait_ge(v_used, TOPK * (n - 1))
                    nc.vector.scalar_tensor_tensor(out=eidx[par][:, :], in0=picked[:, 0, :], scalar=float(K1), in1=picked[:, 1, :],
                                                   op0=ALU.mult, op1=ALU.add).then_inc(topk_step, 1)
                    nc.vector.tensor_scalar(gneg[:, :], top_v[:, 0:1], -1.0, None, ALU.mult).then_inc(topk_step, 1)

            def topk_gates(n, par):
                def after(k):
                    after_topk(n, k)

                dve.wait_ge(gexp_done, n + 1)
                nc.vector.reciprocal(gsum[:, :], gsum[:, :]).then_inc(topk_step, 1)
                after(28)
                nc.vector.tensor_scalar(gate[:, par, :], gexp[:, :], gsum[:, 0:1], None, ALU.mult).then_inc(topk_step, 1)
                after(29)

            def dot(n, par, c):
                dve.wait_ge(u_in[c % U_RING], 16 * (TOPK // U_RING) * n + 16 * (c // U_RING + 1))
                nc.vector.tensor_tensor_reduce(out=u_ring[:, c % U_RING, :], in0=u_ring[:, c % U_RING, :], in1=hn[:, :],
                                               scale=1.0, scalar=0.0, op0=ALU.mult, op1=ALU.add,
                                               accum_out=hid[:, par, c:c + 1]).then_inc(dot_done, 1)

            def dots(n, par, g0):
                for c in range(g0, g0 + COLS):
                    dot(n, par, c)

            def coefs(n, par, g0):
                dve.wait_ge(gelu_done, GRP * n + g0 // COLS + 1)
                nc.vector.tensor_tensor(out=coef[:, par, g0:g0 + COLS], in0=gel[:, par, g0:g0 + COLS],
                                        in1=gate[:, par, g0:g0 + COLS], op=ALU.mult).then_inc(coef_done, 1)

            def add_row(n, par, c):
                dve.wait_ge(v_in[c % V_RING], 16 * (TOPK // V_RING) * n + 16 * (c // V_RING + 1))
                dve.wait_ge(coef_done, GRP * n + c // COLS + 1)
                if n or c:
                    dve.wait_ge(v_used, TOPK * n + c)
                ht = h[:, n // PH, :]
                nc.vector.scalar_tensor_tensor(out=ht, in0=v_ring[:, c % V_RING, :], scalar=coef[:, par, c:c + 1], in1=ht,
                                               op0=ALU.mult, op1=ALU.add).then_inc(v_used, 1)

            def hn_tile(t):
                ht = h[:, t, :] if isinstance(t, int) else h[:, bass.ds(t, 1), :].rearrange("p a n -> p (a n)")
                rt = rstd2[:, t:t + 1] if isinstance(t, int) else rstd2[:, bass.ds(t, 1)]
                nc.vector.scalar_tensor_tensor(out=hn[:, :], in0=ht, scalar=rt, in1=g2b[:, :], op0=ALU.mult, op1=ALU.mult).then_inc(hn_ready, 1)
                dve.wait_ge(hn_ready, t + 1)

            def fin_tile(t):
                dve.wait_ge(v_used, PH * TOPK * (t + 1))
                dve.nop(nofuse=True)
                dve.wait_ge(out_done, 16 * (t + 1))
                dve.nop(nofuse=True)
                for half in range(2):
                    cols = slice(half * BANK, (half + 1) * BANK)
                    ht = h[:, t, cols] if isinstance(t, int) else h[:, bass.ds(t, 1), cols].rearrange("p a n -> p (a n)")
                    nc.vector.tensor_tensor(out=fin[:, cols], in0=acc[half][:, :], in1=ht, op=ALU.add).then_inc(acc_drained, 1)
                dve.wait_ge(acc_drained, 2 * t + 2)
                nc.vector.tensor_tensor_reduce(out=xs[:, :], in0=fin[:, :], in1=fin[:, :], scale=1.0, scalar=0.0,
                                               op0=ALU.mult, op1=ALU.add, accum_out=stat[:, 6:7]).then_inc(fin_step, 1)
                dve.wait_ge(fin_root, t + 1)
                nc.vector.reciprocal(fin_inv[:, :], stat[:, 7:8]).then_inc(fin_step, 1)
                dve.wait_ge(fin_step, FIN * t + 2)
                nc.vector.scalar_tensor_tensor(out=fin[:, :], in0=fin[:, :], scalar=fin_inv[:, 0:1], in1=gfb[:, :],
                                               op0=ALU.mult, op1=ALU.mult).then_inc(fin_step, 1)

            nc.vector.memset(ones[:, :], 1.0)
            nc.vector.memset(ones_row[:, :], 1.0)
            nc.vector.memset(eps[:, :], EPS).then_inc(eps_ready, 1)
            nc.vector.memset(selq[:, :, :], 0.0)
            link(nc.vector.memset(caug[:, :], 0.0))
            dve.wait_ge(pool_const, 6)
            for lo in (0, HD):
                nc.vector.memset(caug[lo + 32:lo + 40, :], 1.0)
                nc.vector.tensor_copy(selq[lo:lo + FH, :, :], ident[0:FH, 0:FH].unsqueeze(2).broadcast_to([FH, FH, P]))
            nc.vector.tensor_copy(iota_f[:, :], iota_i[:, :])
            link(nc.vector.tensor_copy(dist[:, :], fin[:, 0:SEQ].bitcast(I32)))
            link(nc.vector.scalar_tensor_tensor(out=dist[:, :], in0=dist[:, :], scalar=-1.0, in1=dist[:, :], op0=ALU.mult, op1=ALU.max))
            link(nc.vector.tensor_scalar(dist[0:CHUNK, SEQ - CHUNK:SEQ], dist[0:CHUNK, SEQ - CHUNK:SEQ], BIG, None, ALU.add))
            bk = mm_wait(("gain1",))
            nc.vector.tensor_copy(g1c[:, :], bk[:, 0:KC]).then_inc(mm_drained, 1)
            dve.wait_ge(*emptied(("gain1",)))

            for p_ in BEFORE:
                piece(*p_)

            def topk_all(n, par):
                topk_first(n, par)
                for part in range(PARTS):
                    topk_second(n, par, part)
                topk_gates(n, par)

            def next_head(n, par, grp):
                if grp == 0:
                    topk_first(n + 1, 1 - par)
                elif grp == 1:
                    for part in range(PARTS):
                        topk_second(n + 1, 1 - par, part)
                elif grp == 3:
                    topk_gates(n + 1, 1 - par)

            hn_tile(0)
            topk_all(0, 0)
            for tile in range(HOSTS):
                if tile:
                    hn_tile(tile)
                for n in range(PH * tile, PH * tile + PH):
                    par = n % 2
                    for grp in range(GRP):
                        k = GRP * n + grp
                        behind = ((k - 1) // GRP, (k - 1) // GRP % 2, (k - 1) % GRP * COLS)
                        for gap in range(GAPS):
                            c = gap // 2
                            if grp == 1:
                                topk_second(n + 1, 1 - par, gap)
                            elif gap == GAPS - 1:
                                next_head(n, par, grp)
                            if gap % 2 == 0 and gap < GAPS - 1:
                                dot(n, par, grp * COLS + c)
                            elif gap < GAPS - 1 and k > 0:
                                if c == 0:
                                    coefs(*behind)
                                add_row(behind[0], behind[1], behind[2] + c)
                            if k == PH * GRP * tile and gap == GAPS - 1 and tile:
                                fin_tile(tile - 1)
                            for p_ in pieces_in(n, grp, gap):
                                piece(*p_)
                coefs(n, par, grp * COLS)
                for c in range(COLS):
                    add_row(n, par, grp * COLS + c)
                dve.wait_ge(*emptied(MM[-1]))
                dve.wait_ge(*emptied(next(u for u in reversed(MM) if u[0] not in ON_SCALAR)))
                for half in range(2):
                    link(nc.vector.memset(acc[half][:, :], 0.0))
            with dve.Fori(HOSTS, TILES) as t:
                hn_tile(t)
                for par in range(2):
                    for grp in range(GRP):
                        n = PH * t + par
                        dots(n, par, grp * COLS)
                        coefs(n, par, grp * COLS)
                        if par == 0 and grp == 0:
                            fin_tile(t - 1)
                        next_head(n, par, grp)
                with dve.Fori(1, PH // 2) as i:
                    for par in range(2):
                        for grp in range(GRP):
                            n = PH * t + 2 * i + par
                            dots(n, par, grp * COLS)
                            coefs(n, par, grp * COLS)
                            next_head(n, par, grp)
            fin_tile(TILES - 1)


_INS = ['x', 'norm1_g', 'w_in', 'b_f', 'lambda_q1', 'lambda_k1', 'lambda_q2', 'lambda_k2', 'subln_g', 'w_out',
        'norm2_g', 'peer_w_q', 'peer_sub_keys', 'peer_u', 'peer_v', 'final_g']


def kernel(**inputs):
    import numpy as _np
    import concourse.bacc as _bacc
    from concourse import mybir as _mybir
    from concourse.bass_utils import run_bass_kernel_spmd as _run

    nc = _bacc.Bacc("TRN2", target_bir_lowering=False, num_devices=1)
    arrays, args = {}, []
    for name in _INS:
        a = _np.ascontiguousarray(inputs[name])
        arrays[f"in_{name}_dram"] = a
        args.append(nc.dram_tensor(f"in_{name}_dram", a.shape, _mybir.dt.from_np(a.dtype), kind="ExternalInput").ap())
    shape = inputs['x'].shape
    args.append(nc.dram_tensor("out_0_dram", shape, _mybir.dt.from_np(_np.dtype('float32')), kind="ExternalOutput").ap())
    build(nc, *args)
    r = _run(nc, [arrays], core_ids=[0])
    return r.results[0]["out_0_dram"]
```
